# Optimizing a Trainium2 kernel written in Bass

```python
import math
import jax, jax.numpy as jnp
from jax import lax
import numpy as np

D_MODEL = 1024
BATCH = 1
SEQ = 512
DEPTH = 2

CHUNK = 64
EPS = 1e-6
NEG_INF = -1e30
N_NORMS = 6
D_FF = 2816
FFN_RES = 0.5
ROPE_THETA = 10000.0
C_CONV = D_MODEL // 2
CONV_K = 31
H_DIFF = 4
HD_DIFF = 64
DV_DIFF = 2 * HD_DIFF
W_DIFF = H_DIFF * 2 * HD_DIFF
Q_BLOCK = 128
H_CH = 8
HD_CH = 64
W_CH = H_CH * HD_CH
PAST_CHUNKS = 8
BAND = (PAST_CHUNKS + 1) * CHUNK
REL_PAST_MAX = 256
REL_FUT_MAX = CHUNK - 1
N_REL = REL_PAST_MAX + REL_FUT_MAX + 1
N_BRANCH = 3
OFF_GLU = 0
OFF_DQ = OFF_GLU + 2 * C_CONV
OFF_DK = OFF_DQ + W_DIFF
OFF_DV = OFF_DK + W_DIFF
OFF_CQ = OFF_DV + W_DIFF
OFF_CK = OFF_CQ + W_CH
OFF_CV = OFF_CK + W_CH
OFF_GATE = OFF_CV + W_CH
D_IN = OFF_GATE + N_BRANCH * D_MODEL

kernel_name = "hybrid_gated_conv_diffattn_chunkattn_macaron"

def rmsnorm(x, g):
    xf = x.astype(jnp.float32)
    y = xf * lax.rsqrt(jnp.mean(xf * xf, axis=-1, keepdims=True) + EPS)
    return (y * g.astype(jnp.float32)).astype(x.dtype)

def layernorm(x, g, b):
    xf = x.astype(jnp.float32)
    mu = jnp.mean(xf, axis=-1, keepdims=True)
    var = jnp.mean(jnp.square(xf - mu), axis=-1, keepdims=True)
    y = (xf - mu) * lax.rsqrt(var + EPS)
    return (y * g.astype(jnp.float32) + b.astype(jnp.float32)).astype(x.dtype)

def swiglu(h, w_in, w_out):
    gate, up = jnp.split(h @ w_in, 2, axis=-1)
    return (jax.nn.silu(gate) * up) @ w_out

def rope(t, cos, sin):
    half = t.shape[-1] // 2
    c = cos[None, :, None, None, :]
    s = sin[None, :, None, None, :]
    t1, t2 = t[..., :half], t[..., half:]
    return jnp.concatenate([t1 * c - t2 * s, t2 * c + t1 * s], axis=-1)

def conv_module(u, dw, db, ln_g, ln_b, w_out):
    a, b = jnp.split(u, 2, axis=-1)
    z = a * jax.nn.sigmoid(b)
    z = lax.conv_general_dilated(z, dw[:, None, :], window_strides=(1,),
                                 padding=[(CONV_K - 1, 0)],
                                 dimension_numbers=('NWC', 'WIO', 'NWC'),
                                 feature_group_count=C_CONV) + db
    z = jax.nn.silu(layernorm(z, ln_g, ln_b))
    return z @ w_out

def diff_attention(q, k, v, lam, lam_init):
    B, S = q.shape[0], q.shape[1]
    nqb = S // Q_BLOCK
    scale = HD_DIFF ** -0.5
    kchunk = jnp.arange(S) // CHUNK
    qb = jnp.moveaxis(q.reshape(B, nqb, Q_BLOCK, H_DIFF, 2, HD_DIFF), 1, 0)

    def block(args):
        qi, idx = args
        s = jnp.einsum('bqhcd,bkhcd->bhcqk', qi, k).astype(jnp.float32) * scale
        qchunk = (idx * Q_BLOCK + jnp.arange(Q_BLOCK)) // CHUNK
        mask = kchunk[None, :] <= qchunk[:, None]
        p = jax.nn.softmax(jnp.where(mask, s, NEG_INF), axis=-1)
        a = p[:, :, 0] - lam * p[:, :, 1]
        return jnp.einsum('bhqk,bkhe->bqhe', a.astype(v.dtype), v)

    o = lax.map(block, (qb, jnp.arange(nqb)))
    o = jnp.moveaxis(o, 0, 1).reshape(B, S, H_DIFF, DV_DIFF)
    of = o.astype(jnp.float32)
    of = of * lax.rsqrt(jnp.mean(of * of, axis=-1, keepdims=True) + EPS)
    return (of * (1.0 - lam_init)).astype(v.dtype).reshape(B, S, W_DIFF)

def chunk_attention(q, k, v, rel_bias):
    B, S = q.shape[0], q.shape[1]
    nc = S // CHUNK
    pad = PAST_CHUNKS * CHUNK
    kp = jnp.pad(k, ((0, 0), (pad, 0), (0, 0), (0, 0)))
    vp = jnp.pad(v, ((0, 0), (pad, 0), (0, 0), (0, 0)))
    i = jnp.arange(CHUNK)[:, None]
    r = jnp.arange(BAND)[None, :]
    rel = jnp.clip(i - r + pad, -REL_FUT_MAX, REL_PAST_MAX) + REL_FUT_MAX
    bias = rel_bias[:, rel].astype(jnp.float32)
    scale = HD_CH ** -0.5

    def one(c):
        qc = lax.dynamic_slice_in_dim(q, c * CHUNK, CHUNK, axis=1)
        kc = lax.dynamic_slice_in_dim(kp, c * CHUNK, BAND, axis=1)
        vc = lax.dynamic_slice_in_dim(vp, c * CHUNK, BAND, axis=1)
        s = jnp.einsum('bqhd,bkhd->bhqk', qc, kc).astype(jnp.float32) * scale + bias
        valid = (c - PAST_CHUNKS) * CHUNK + jnp.arange(BAND) >= 0
        p = jax.nn.softmax(jnp.where(valid, s, NEG_INF), axis=-1)
        return jnp.einsum('bhqk,bkhd->bqhd', p.astype(v.dtype), vc)

    o = lax.map(one, jnp.arange(nc))
    return jnp.moveaxis(o, 0, 1).reshape(B, S, W_CH)

def setup_inputs(seed: int = 0) -> dict:
    key = jax.random.key(seed)
    ks = jax.random.split(key, 24)
    f32 = jnp.float32

    def w(k, shape, fan_in):
        return jax.random.normal(k, shape, f32) * fan_in ** -0.5

    x = jax.random.normal(ks[0], (BATCH, SEQ, D_MODEL), f32)
    norm_g = 1.0 + 0.05 * jax.random.normal(ks[1], (DEPTH, N_NORMS, D_MODEL), f32)
    ffn1_in = w(ks[2], (DEPTH, D_MODEL, 2 * D_FF), D_MODEL)
    ffn1_out = w(ks[3], (DEPTH, D_FF, D_MODEL), D_FF)
    w_in = w(ks[4], (DEPTH, D_MODEL, D_IN), D_MODEL)
    gate_b = 0.1 * jax.random.normal(ks[5], (DEPTH, N_BRANCH * D_MODEL), f32)
    conv_dw = w(ks[6], (DEPTH, CONV_K, C_CONV), CONV_K)
    conv_b = 0.02 * jax.random.normal(ks[7], (DEPTH, C_CONV), f32)
    conv_ln = jnp.stack([1.0 + 0.05 * jax.random.normal(ks[8], (DEPTH, C_CONV), f32),
                         0.02 * jax.random.normal(ks[9], (DEPTH, C_CONV), f32)], axis=1)
    w_conv_out = w(ks[10], (DEPTH, C_CONV, D_MODEL), C_CONV)
    diff_lambda = 0.1 * jax.random.normal(ks[11], (DEPTH, 4, HD_DIFF), f32)
    w_diff_out = w(ks[12], (DEPTH, W_DIFF, D_MODEL), W_DIFF)
    rel_bias = 0.2 * jax.random.normal(ks[13], (DEPTH, H_CH, N_REL), f32)
    w_chunk_out = w(ks[14], (DEPTH, W_CH, D_MODEL), W_CH)
    w_o = w(ks[15], (DEPTH, D_MODEL, D_MODEL), D_MODEL)
    ffn2_in = w(ks[16], (DEPTH, D_MODEL, 2 * D_FF), D_MODEL)
    ffn2_out = w(ks[17], (DEPTH, D_FF, D_MODEL), D_FF)
    return {"x": x, "norm_g": norm_g, "ffn1_in": ffn1_in, "ffn1_out": ffn1_out,
            "w_in": w_in, "gate_b": gate_b, "conv_dw": conv_dw, "conv_b": conv_b,
            "conv_ln": conv_ln, "w_conv_out": w_conv_out, "diff_lambda": diff_lambda,
            "w_diff_out": w_diff_out, "rel_bias": rel_bias, "w_chunk_out": w_chunk_out,
            "w_o": w_o, "ffn2_in": ffn2_in, "ffn2_out": ffn2_out}

def reference(x, norm_g, ffn1_in, ffn1_out, w_in, gate_b, conv_dw, conv_b, conv_ln,
              w_conv_out, diff_lambda, w_diff_out, rel_bias, w_chunk_out, w_o,
              ffn2_in, ffn2_out):
    B, S, D = x.shape
    pos = jnp.arange(S, dtype=jnp.float32)
    inv_freq = ROPE_THETA ** (-jnp.arange(0, HD_DIFF, 2, dtype=jnp.float32) / HD_DIFF)
    ang = pos[:, None] * inv_freq[None, :]
    cos = jnp.cos(ang).astype(x.dtype)
    sin = jnp.sin(ang).astype(x.dtype)

    for l in range(DEPTH):
        g = norm_g[l]
        x = x + FFN_RES * rmsnorm(swiglu(rmsnorm(x, g[0]), ffn1_in[l], ffn1_out[l]), g[1])

        h = rmsnorm(x, g[2])
        p = h @ w_in[l]
        y_a = conv_module(p[..., OFF_GLU:OFF_DQ], conv_dw[l], conv_b[l],
                          conv_ln[l, 0], conv_ln[l, 1], w_conv_out[l])
        dq = rope(p[..., OFF_DQ:OFF_DK].reshape(B, S, H_DIFF, 2, HD_DIFF), cos, sin)
        dk = rope(p[..., OFF_DK:OFF_DV].reshape(B, S, H_DIFF, 2, HD_DIFF), cos, sin)
        dv = p[..., OFF_DV:OFF_CQ].reshape(B, S, H_DIFF, DV_DIFF)
        lam_init = 0.8 - 0.6 * math.exp(-0.3 * l)
        lamp = diff_lambda[l].astype(jnp.float32)
        lam = (jnp.exp(jnp.sum(lamp[0] * lamp[1])) - jnp.exp(jnp.sum(lamp[2] * lamp[3]))
               + lam_init)
        y_b = diff_attention(dq, dk, dv, lam, lam_init) @ w_diff_out[l]
        cq = p[..., OFF_CQ:OFF_CK].reshape(B, S, H_CH, HD_CH)
        ck = p[..., OFF_CK:OFF_CV].reshape(B, S, H_CH, HD_CH)
        cv = p[..., OFF_CV:OFF_GATE].reshape(B, S, H_CH, HD_CH)
        y_c = chunk_attention(cq, ck, cv, rel_bias[l]) @ w_chunk_out[l]
        gates = jax.nn.sigmoid(p[..., OFF_GATE:] + gate_b[l]).reshape(B, S, N_BRANCH, D)
        mix = gates[:, :, 0] * y_a + gates[:, :, 1] * y_b + gates[:, :, 2] * y_c
        x = x + rmsnorm(mix @ w_o[l], g[3])

        x = x + FFN_RES * rmsnorm(swiglu(rmsnorm(x, g[4]), ffn2_in[l], ffn2_out[l]), g[5])
    return x


_drawn_inputs = setup_inputs


def setup_inputs(seed=0):
    import zlib

    import numpy as np

    out = dict(_drawn_inputs(seed))
    spreads = {}
    factors = {}
    for name, (base, spread) in spreads.items():
        noise = np.random.default_rng([zlib.crc32(name.encode()), seed]).standard_normal(out[name].shape)
        drawn = base * np.exp(spread * noise) if base else spread * noise
        out[name] = __import__('jax').numpy.asarray(drawn.astype(out[name].dtype))
    for name, factor in factors.items():
        out[name] = (out[name] * factor).astype(out[name].dtype)
    return out
```

```python
import math
from contextlib import ExitStack

import numpy as np

import concourse.bass as bass
from concourse import mybir

ACT = mybir.ActivationFunctionType
ALU = mybir.AluOpType
AX = mybir.AxisListType
F32 = mybir.dt.float32
F32R = mybir.dt.float32r

P = 128
D_MODEL = 1024
SEQ = 512
DEPTH = 2
D_FF = 2816
C_CONV = 512
CONV_K = 31
EPS = 1e-6
REL_PAST = 256
N_REL = 320
HEADS_CHUNK = 8
ATT_SCALE = 64 ** -0.5

KD = D_MODEL // P
KF = D_FF // P
KC = C_CONV // P
TT = SEQ // P
RING = 4
CHUNK = KD * P
FFN_OUT_K = (6, 6, 5, 5)
FFN_OUT_AT = (0, 6, 12, 17, 22)

C_FFN1_IN = 0
C_FFN1_OUT = C_FFN1_IN + 2 * KF
C_GLU = C_FFN1_OUT + 4 * KD
C_DQK = C_GLU + 2 * KC
C_DV = C_DQK + 2 * KC
C_A = C_DV + 4
C_CQK = C_A + 2 * KD
C_CV = C_CQK + 2 * KC
C_B = C_CV + 4
C_C = C_B + 2 * KD
C_WO = C_C + 2 * KD
C_FFN2_IN = C_WO + KD
C_FFN2_OUT = C_FFN2_IN + 2 * KF
CHUNKS = C_FFN2_OUT + 4 * KD
assert CHUNKS == 240 and all(c % RING == 0 for c in (C_FFN1_OUT, C_GLU, C_DQK, C_DV, C_A, C_CQK, C_CV, C_B, C_C, C_WO, C_FFN2_IN, C_FFN2_OUT))


def chunk_cols(n):
    if C_FFN1_OUT <= n < C_GLU or C_FFN2_OUT <= n < CHUNKS:
        return FFN_OUT_K[n % RING] * P
    if C_A <= n < C_CQK or C_B <= n < C_WO:
        return KD * P if n % 2 == 0 else KC * P
    return KD * P


PAR_NORM = 0
PAR_GATE_B = PAR_NORM + 6 * KD
PAR_DW = PAR_GATE_B + 3 * KD
PAR_CONV_B = PAR_DW + KC * CONV_K
PAR_LN = PAR_CONV_B + KC
N_PAR = PAR_LN + 2 * KC

PHASES = (C_FFN1_IN, C_FFN1_OUT, C_GLU, C_A, C_CQK, C_B, C_WO, C_FFN2_IN, C_FFN2_OUT, CHUNKS)
N_CONSTS = 3 + DEPTH + 4
NEG_R = -2.0 ** 100


def lam_init(l):
    return 0.8 - 0.6 * math.exp(-0.3 * l)


EXT_LEFT = 256
EXT = EXT_LEFT + N_REL + 64


class Signal:

    def __init__(self, sem, per_layer, credit=0):
        self.sem, self.per_layer, self.credit = sem, per_layer, credit

    def at(self, lay, k):
        return lay * self.per_layer + (k + self.credit)



def build(nc, xT, ffn_in, ffn_out, mix_in, br_out, wo, par, lamb, relb, rope, outT):
    with ExitStack() as ctx:
        def sb(name, shape, dt=F32):
            return ctx.enter_context(nc.sbuf_tensor(name, shape, dt))

        def bank(name):
            return ctx.enter_context(nc.psum_tensor(name, [P, SEQ], F32))

        def sig(name, per_layer, credit=0):
            return Signal(ctx.enter_context(nc.semaphore(name)), per_layer, credit)

        region_at = (nc.sbuf_base + 31) // 32 * 32
        region = sb("region", [P, 2 * KF * SEQ])

        def at(name, offset, shape, dt=F32):
            return nc.alloc_sbuf_tensor_at(name, [P, *shape], dt, offset=region_at + offset)

        TILE = 4 * SEQ
        act_hi = at("act_hi", 0, [KF, SEQ], F32R)
        act_lo = at("act_lo", KF * TILE, [KF, SEQ], F32R)
        q_all = at("q_all", 0, [KC, SEQ])
        k_all = at("k_all", 4 * TILE, [KC, SEQ])
        v_all = at("v_all", 8 * TILE, [TT, SEQ])
        u_hi = at("u_hi", 12 * TILE, [KC, SEQ], F32R)
        u_lo = at("u_lo", 16 * TILE, [KC, SEQ], F32R)
        v_raw = at("v_raw", 20 * TILE, [KC, SEQ])
        v_sq = at("v_sq", 24 * TILE, [KC, SEQ])
        v_hi = at("v_hi", 20 * TILE, [KC, SEQ], F32R)
        v_lo = at("v_lo", 24 * TILE, [KC, SEQ], F32R)
        ZPAD = CONV_K - 1
        z = at("z", 28 * TILE, [KC, ZPAD + SEQ])
        conv_odd = at("conv_odd", 33 * TILE, [SEQ])
        q_hi = at("q_hi", 28 * TILE, [SEQ], F32R)
        q_lo = at("q_lo", 29 * TILE, [SEQ], F32R)
        k_hi = at("k_hi", 30 * TILE, [SEQ], F32R)
        k_lo = at("k_lo", 31 * TILE, [SEQ], F32R)
        val_hi = at("val_hi", 32 * TILE, [2, TT, P], F32R)
        val_lo = at("val_lo", 34 * TILE, [2, TT, P], F32R)
        prob = at("prob", 36 * TILE, [2, 2, SEQ])
        pt_hi = at("pt_hi", 40 * TILE, [2, TT, P], F32R)
        pt_lo = at("pt_lo", 42 * TILE, [2, TT, P], F32R)
        mix_hi = at("mix_hi", 28 * TILE, [KD, SEQ], F32R)
        mix_lo = at("mix_lo", 36 * TILE, [KD, SEQ], F32R)

        x = sb("x", [P, KD, SEQ])
        h_hi = sb("h_hi", [P, KD, SEQ], F32R)
        h_lo = sb("h_lo", [P, KD, SEQ], F32R)
        raw = sb("raw", [P, RING, CHUNK])
        w_hi = sb("w_hi", [P, RING, CHUNK], F32R)
        w_lo = sb("w_lo", [P, RING, CHUNK], F32R)
        ymix = sb("ymix", [P, KD, SEQ])
        strip = sb("strip", [P, 2, SEQ])
        ident = sb("ident", [P, P])
        ones = sb("ones", [P, P])
        rbc = sb("rbc", [P, SEQ])
        sqacc = sb("sqacc", [P, SEQ])
        diag = sb("diag", [P, TT, P])
        tmp = [sb(f"tmp{i}", [P, SEQ]) for i in range(4)]
        par_all = sb("par_all", [P, DEPTH, N_PAR])
        pr = sb("pr", [P, N_PAR])
        mask_q = sb("mask_q", [P, P], F32R)
        mask_k = sb("mask_k", [P, P // 2], F32R)
        small = sb("small", [P, 64])
        std = small[:, 0:4]
        rtok = small[:, 4:8]
        std2 = small[:, 8:24]
        rtok2 = small[:, 24:40]

        def negmax(par_, c):
            return small[:, 40 + 2 * par_ + c:41 + 2 * par_ + c]

        def rowsum(par_, c):
            return small[:, 44 + 2 * par_ + c:45 + 2 * par_ + c]

        rinv = small[:, 48:50]
        lam_r1 = small[:, 50:51]
        lam_exp = small[:, 52:52 + 2 * DEPTH]
        neg_lam = small[:, 56:56 + DEPTH]
        out_scale = small[:, 58:58 + DEPTH]
        eps_col = small[:, 60:61]

        acc = [bank(f"acc{i}") for i in range(4)]
        sc = [bank(f"sc{i}") for i in range(2)]
        tr = bank("tr")
        pv = bank("pv")

        ext = nc.dram_tensor("ext", [DEPTH * HEADS_CHUNK, P, EXT], F32, kind="Internal")

        x_landed = sig("x_landed", 0)
        par_landed = sig("par_landed", 0)
        lam_landed = sig("lam_landed", 0)
        rel_landed = sig("rel_landed", 0)
        ext_stored = sig("ext_stored", 0)
        out_stored = sig("out_stored", 0)
        zeroed = sig("zeroed", 0)
        consts = sig("consts", 0)
        rel_ready = sig("rel_ready", 0)
        setup = sig("setup", 0)
        lam_prod = sig("lam_prod", 0)
        lam_done = sig("lam_done", 0)
        landed = [sig(f"landed{i}", 16 * CHUNKS // RING) for i in range(RING)]
        tables_landed = sig("tables_landed", 32)
        strip_landed = sig("strip_landed", 16 * KC)

        hi_done = sig("hi_done", CHUNKS)
        split_done = sig("split_done", CHUNKS, RING)
        chunk_used = sig("chunk_used", CHUNKS, RING)

        par_copied = sig("par_copied", 4)
        pair_scaled = sig("pair_scaled", 4 * KF + 2 * KC, 4)
        gate_act = sig("gate_act", 2 * KF + KC)
        act_raw = sig("act_raw", 2 * KF)
        act_hi_done = sig("act_hi_done", 2 * KF)
        act_ready = sig("act_ready", 2 * KF)
        y_evicted = sig("y_evicted", 3 * KD, 2)
        squared = sig("squared", 3 * KD)
        sq_added = sig("sq_added", 6 * KD)
        summed = sig("summed", 6)
        std_ready = sig("std_ready", 6)
        rtok_ready = sig("rtok_ready", 6)
        diag_ready = sig("diag_ready", 6)
        bcast = sig("bcast", 6)
        rbc_ready = sig("rbc_ready", 6)
        x_scaled = sig("x_scaled", 3 * KD)
        x_ready = sig("x_ready", 3 * KD)
        h_hi_done = sig("h_hi_done", 3 * KD)
        h_ready = sig("h_ready", 3 * KD)

        z_padded = sig("z_padded", 1)
        z_ready = sig("z_ready", KC)
        tap_done = sig("tap_done", KC * (CONV_K + 1))
        tables_ready = sig("tables_ready", 2)
        swapped = sig("swapped", 2 * KC)
        cos_part = sig("cos_part", 2 * KC)
        sin_part = sig("sin_part", 2 * KC)
        rope_done = sig("rope_done", 2 * KC)
        v_evicted = sig("v_evicted", 2 * TT)
        cqk_evicted = sig("cqk_evicted", 2 * KC)
        ln_sums = sig("ln_sums", 2)
        ln_mean = sig("ln_mean", 1)
        ln_std = sig("ln_std", 1)
        ln_rstd = sig("ln_rstd", 1)
        ln_diag = sig("ln_diag", 2)
        ln_bcast = sig("ln_bcast", 2)
        ln_centred = sig("ln_centred", KC)
        ln_squared = sig("ln_squared", KC)
        ln_normed = sig("ln_normed", KC)
        conv_act = sig("conv_act", KC)
        conv_hi = sig("conv_hi", KC)
        u_ready = sig("u_ready", 2 * KC)

        val_zeroed = sig("val_zeroed", 1)
        qk_hi_done = sig("qk_hi_done", 2 * KC)
        qk_staged = sig("qk_staged", 2 * KC)
        val_hi_done = sig("val_hi_done", 2 * KC)
        val_staged = sig("val_staged", 2 * KC)
        scores_done = sig("scores_done", 4 * 16)
        neg_ready = sig("neg_ready", 4 * 16)
        exp_done = sig("exp_done", 4 * 16, 2)
        row_steps = sig("row_steps", 3 * 16 + 16)
        prob_ready = sig("prob_ready", 2 * 16)
        turned = sig("turned", 16 + 32)
        pt_hi_done = sig("pt_hi_done", 16 + 32)
        pt_ready = sig("pt_ready", 16 + 32, 1)
        pv_done = sig("pv_done", 2 * 16, 1)
        o_hi_done = sig("o_hi_done", KC)
        o_evicted = sig("o_evicted", 2 * KC, 1)
        dn_sums = sig("dn_sums", 1)
        dn_std = sig("dn_std", 1)
        dn_rtok = sig("dn_rtok", 2)
        dn_diag = sig("dn_diag", KC)
        dn_bcast = sig("dn_bcast", KC)
        dn_normed = sig("dn_normed", KC)
        dn_hi = sig("dn_hi", KC)

        gate_evicted = sig("gate_evicted", 3 * KD, 2)
        gate_tanh = sig("gate_tanh", 3 * KD)
        out_evicted = sig("out_evicted", 3 * KD, 2)
        mix_added = sig("mix_added", 2 * KD)
        mix_hi_done = sig("mix_hi_done", KD)
        mix_ready = sig("mix_ready", KD)

        block = ctx.enter_context(nc.Block())

        @block.sync
        def _(sp):
            def fetch(lay, n, s, src):
                sp.wait_ge(split_done.sem, split_done.at(lay, n + 1 - RING))
                sp.dma_start(raw[:, s, 0:src.shape[-1]], src).then_inc(landed[s].sem, 16)

            def fetch_ffn(lay, which, c_in, c_out):
                with sp.Fori(0, 2 * KF // RING) as i:
                    for s in range(RING):
                        fetch(lay, c_in + i * RING + s, s, ffn_in[(lay * 2 + which) * (2 * KF) + i * RING + s])
                with sp.Fori(0, KD) as t:
                    for s, (a, b) in enumerate(zip(FFN_OUT_AT[:-1], FFN_OUT_AT[1:])):
                        fetch(lay, c_out + t * RING + s, s, ffn_out[(lay * 2 + which) * KD + t, :, a * P:b * P])

            def fetch_mix(lay, c, n, first):
                with sp.Fori(0, n // RING) as i:
                    for s in range(RING):
                        fetch(lay, c + i * RING + s, s, mix_in[lay * 56 + first + i * RING + s])

            def fetch_gate_out(lay, c, gate_first, branch, strips=False):
                with sp.Fori(0, KC) as g:
                    for s in range(RING):
                        src = mix_in[lay * 56 + gate_first + g * 2 + s // 2] if s % 2 == 0 else \
                            br_out[lay * (3 * KD) + branch * KD + g * 2 + s // 2]
                        fetch(lay, c + g * RING + s, s, src)
                    if strips:
                        sp.wait_ge(neg_ready.sem, neg_ready.at(lay, 32 + g * 8))
                        sp.dma_start(strip[:, :, :], bass.AP(
                            ext, (lay * HEADS_CHUNK + g * 2) * (P * EXT) + P,
                            [[EXT - 1, P], [P * EXT, 2], [1, SEQ]])).then_inc(strip_landed.sem, 16)

            sp.dma_start(x[:, :, :], xT).then_inc(x_landed.sem, 16)
            sp.dma_start(par_all[:, :, :], par).then_inc(par_landed.sem, 16)
            sp.dma_start(ymix[0:DEPTH * HEADS_CHUNK, 0:2, :].rearrange("p a b -> p (a b)")[:, EXT_LEFT:EXT_LEFT + N_REL],
                         relb).then_inc(rel_landed.sem, 16)
            sp.dma_start(tmp[0][:, :], lamb.partition_broadcast(P)).then_inc(lam_landed.sem, 16)
            sp.wait_ge(rel_ready.sem, 2)
            row = ymix[0:DEPTH * HEADS_CHUNK, 0:2, :].rearrange("p a b -> p (a b)")[:, 0:EXT]
            sp.dma_start(ext.ap(), row.unsqueeze(1).to_broadcast([DEPTH * HEADS_CHUNK, P, EXT])).then_inc(ext_stored.sem, 16)

            with sp.Fori(0, DEPTH) as lay:
                fetch_ffn(lay, 0, C_FFN1_IN, C_FFN1_OUT)
                fetch_mix(lay, C_GLU, 2 * KC, 0)
                sp.wait_ge(x_ready.sem, x_ready.at(lay, KD))
                for i in range(2):
                    sp.dma_start(ymix[:, i, :], rope[i]).then_inc(tables_landed.sem, 16)
                fetch_mix(lay, C_DQK, 12, 8)
                fetch_gate_out(lay, C_A, 20, 0)
                fetch_mix(lay, C_CQK, 12, 28)
                sp.wait_ge(ext_stored.sem, 16)
                fetch_gate_out(lay, C_B, 40, 1, strips=True)
                fetch_gate_out(lay, C_C, 48, 2)
                with sp.Fori(0, KD // RING) as i:
                    for s in range(RING):
                        fetch(lay, C_WO + i * RING + s, s, wo[lay * KD + i * RING + s])
                fetch_ffn(lay, 1, C_FFN2_IN, C_FFN2_OUT)
            for t in range(KD):
                sp.wait_ge(x_ready.sem, x_ready.at(DEPTH - 1, 2 * KD + t + 1))
                sp.dma_start(outT[:, t, :], x[:, t, :]).then_inc(out_stored.sem, 16)
            sp.wait_ge(out_stored.sem, 16 * KD)

        @block.gpsimd
        def _(pool):
            pool.memset(ident[:, :], 0.0).then_inc(zeroed.sem, 1)
            pool.memset(ones[:, :], 1.0).then_inc(consts.sem, 1)
            pool.memset(mask_q[:, :].bitcast(F32), 0.0).then_inc(zeroed.sem, 1)
            pool.memset(mask_k[:, :].bitcast(F32), 0.0).then_inc(zeroed.sem, 1)
            pool.memset(eps_col, EPS).then_inc(consts.sem, 1)
            for l in range(DEPTH):
                pool.memset(out_scale[:, l:l + 1], 1.0 - lam_init(l)).then_inc(consts.sem, 1)
            pool.wait_ge(zeroed.sem, 3)
            pool.affine_select(out=ident[:, :], in_=ident[:, :], compare_op=ALU.not_equal, fill=1.0, base=0,
                               pattern=[[-1, P]], channel_multiplier=1).then_inc(consts.sem, 1)

            def split_lo(lay, n, s, cols):
                pool.wait_ge(hi_done.sem, hi_done.at(lay, n + 1))
                pool.tensor_tensor(w_lo[:, s, 0:cols], raw[:, s, 0:cols], w_hi[:, s, 0:cols].bitcast(F32),
                                   ALU.subtract).then_inc(split_done.sem, 1)

            pool.sem_inc(split_done.sem, RING)
            with pool.Fori(0, DEPTH) as lay:
                for a, b in zip(PHASES[:-1], PHASES[1:]):
                    with pool.Fori(0, (b - a) // RING) as i:
                        for s in range(RING):
                            split_lo(lay, a + i * RING + s, s, chunk_cols(a + s))


        @block.scalar
        def _(act):
            def split_hi(lay, n, s, cols):
                act.wait_ge(landed[s].sem, landed[s].at(lay, n_round(n) * 16 + 16))
                act.wait_ge(chunk_used.sem, chunk_used.at(lay, chunk_at(n) + 1 - RING))
                act.activation(w_hi[:, s, 0:cols], raw[:, s, 0:cols], ACT.Copy).then_inc(hi_done.sem, 1)

            def n_round(n):
                return n // RING if isinstance(n, int) else n[1] + (n[0] + n[2]) // RING

            def chunk_at(n):
                return n if isinstance(n, int) else n[1] * RING + (n[0] + n[2])

            def ahead(lay, c, i, s, last):
                m = s + RING - 1
                if last:
                    n = c + i * RING + m
                    if n < CHUNKS:
                        split_hi(lay, n, n % RING, chunk_cols(n))
                else:
                    split_hi(lay, (c, i, m), m % RING, chunk_cols(c + m))

            def norm_tail(lay, k):
                act.wait_ge(summed.sem, summed.at(lay, k + 1))
                act.activation(std, pv[:, 0:TT], ACT.Sqrt, bias=eps_col, scale=1.0 / D_MODEL).then_inc(std_ready.sem, 1)
                act.wait_ge(bcast.sem, bcast.at(lay, k + 1))
                act.activation(rbc[:, :], tr[:, :], ACT.Copy).then_inc(rbc_ready.sem, 1)

            def squares(lay, sub, t, src):
                if t >= 2:
                    act.wait_ge(sq_added.sem, sq_added.at(lay, 2 * sub * KD + t - 1))
                act.activation(tmp[2 + t % 2][:, :], src, ACT.Square).then_inc(squared.sem, 1)

            def norm_head(lay, sub, fresh):
                g = (0, 2, 4)[sub]
                for t in range(KD):
                    if fresh:
                        act.wait_ge(x_ready.sem, x_ready.at(lay, (sub - 1) * KD + t + 1))
                    act.activation(h_hi[:, t, :], x[:, t, :], ACT.Copy, scale=pr[:, g * KD + t:g * KD + t + 1])\
                        .then_inc(h_hi_done.sem, 1)
                for t in range(KD):
                    squares(lay, sub, t, x[:, t, :])

            def pairs(lay, c, first_pair, n_pairs, k_norm):
                ffn = n_pairs == KF
                which = 0 if c == C_FFN1_IN else 1

                def pair(i, last, s, j):
                    ahead(lay, c, i, s, last)
                    if k_norm is not None and isinstance(j, int) and j == 0:
                        norm_tail(lay, k_norm)
                    p = first_pair + j
                    act.wait_ge(pair_scaled.sem, pair_scaled.at(lay, 2 * p + 1))
                    if ffn:
                        act.activation(tmp[1][:, :], tmp[0][:, :], ACT.Silu).then_inc(gate_act.sem, 1)
                    else:
                        if j >= 1:
                            act.wait_ge(z_ready.sem, z_ready.at(lay, j))
                        act.activation(tmp[1][:, :], tmp[0][:, :], ACT.Sigmoid).then_inc(gate_act.sem, 1)
                    ahead(lay, c, i, s + 1, last)
                    if ffn:
                        act.wait_ge(act_raw.sem, act_raw.at(lay, which * KF + j + 1))
                        act.activation(act_hi[:, j, :], tmp[3][:, :], ACT.Copy).then_inc(act_hi_done.sem, 1)

                n = n_pairs // 2
                pair(0, n == 1, 0, 0)
                pair(0, n == 1, 2, 1)
                if n > 2:
                    with act.Fori(1, n - 1) as i:
                        pair(i, False, 0, i * 2)
                        pair(i, False, 2, i * 2 + 1)
                pair(n - 1, True, 0, 2 * n - 2)
                pair(n - 1, True, 2, 2 * n - 1)

            def y_tile(lay, sub, t, bank_, n_used, parity):
                act.wait_ge(chunk_used.sem, chunk_used.at(lay, n_used))
                act.activation(ymix[:, t, :], bank_[:, :], ACT.Copy)
                if not isinstance(t, int) or t >= 2:
                    act.wait_ge(sq_added.sem, sq_added.at(lay, (2 * sub + 1) * KD + t - 1))
                act.activation(tmp[2 + parity][:, :], bank_[:, :], ACT.Square).then_inc(y_evicted.sem, 1)

            def ffn_out_tiles(lay, sub, c):
                def two(i, last, t):
                    for s in range(2 * RING):
                        ahead(lay, c, i * 2, s, last)
                        if s % RING == RING - 1:
                            y_tile(lay, sub, t + s // RING, acc[s // RING], c + RING + t * RING + s // RING * RING,
                                   s // RING)
                two(0, False, 0)
                with act.Fori(1, KD // 2 - 1) as i:
                    two(i, False, i * 2)
                two(KD // 2 - 1, True, KD - 2)

            def rope_swap(lay, j, bank_, scale, n):
                act.wait_ge(chunk_used.sem, chunk_used.at(lay, n + 1))
                if j >= 2:
                    act.wait_ge(rope_done.sem, rope_done.at(lay, j - 1))
                else:
                    act.wait_ge(z_ready.sem, z_ready.at(lay, KC))
                for g in range(4):
                    o = act.activation(tmp[j % 2][32 * (g ^ 1):32 * (g ^ 1) + 32, :],
                                       bank_[32 * g:32 * g + 32, :], ACT.Copy, scale=scale)
                o.then_inc(swapped.sem, 1)

            def values(lay, c):
                for s in range(RING):
                    ahead(lay, c, 0, s, True)
                act.wait_ge(chunk_used.sem, chunk_used.at(lay, c + RING))
                for t in range(TT):
                    act.activation(v_all[:, t, :], acc[t][:, :], ACT.Copy, scale=rtok[:, t:t + 1])\
                        .then_inc(v_evicted.sem, 1)

            def conv_norm(lay):
                for t in range(KC):
                    act.wait_ge(ln_centred.sem, ln_centred.at(lay, t + 1))
                    act.activation(v_sq[:, t, :], v_raw[:, t, :], ACT.Square).then_inc(ln_squared.sem, 1)
                act.wait_ge(ln_sums.sem, ln_sums.at(lay, 2))
                act.activation(std2[:, 0:TT], pv[:, 0:TT], ACT.Sqrt, bias=eps_col, scale=1.0 / C_CONV)\
                    .then_inc(ln_std.sem, 1)
                for t in range(KC):
                    act.wait_ge(ln_normed.sem, ln_normed.at(lay, t + 1))
                    act.activation(v_sq[:, t, :], v_raw[:, t, :], ACT.Silu, bias=pr[:, PAR_LN + KC + t:PAR_LN + KC + t + 1],
                                   scale=pr[:, PAR_LN + t:PAR_LN + t + 1]).then_inc(conv_act.sem, 1)
                for t in range(KC):
                    act.wait_ge(conv_act.sem, conv_act.at(lay, t + 1))
                    act.activation(u_hi[:, t, :], v_sq[:, t, :], ACT.Copy).then_inc(conv_hi.sem, 1)

            def diff_norm(lay):
                act.wait_ge(dn_sums.sem, dn_sums.at(lay, 1))
                act.activation(std2, pv[:, 0:16], ACT.Sqrt, bias=eps_col, scale=1.0 / P).then_inc(dn_std.sem, 1)

            def attention(lay, kind, c, branch):
                U0, H0, S0, T0 = 16 * kind, KC * kind, 32 * kind, 16 * kind
                n_comp = 1 + kind

                def turn_unit(h, u):
                    hp, up = (h, u - 1) if u else (h - 1, 3)
                    for comp in range(n_comp):
                        m = T0 + n_comp * (hp * 4 + up) + comp
                        act.wait_ge(turned.sem, turned.at(lay, m + 1))
                        act.wait_ge(pv_done.sem, pv_done.at(lay, U0 + hp * 4 + up))
                        w = (up + 1) * P
                        act.activation(pt_hi[:, comp, 0:up + 1, :].rearrange("p a b -> p (a b)"), tr[:, 0:w], ACT.Copy)\
                            .then_inc(pt_hi_done.sem, 1)

                def outputs(hp):
                    act.wait_ge(pv_done.sem, pv_done.at(lay, U0 + hp * 4 + 4))
                    if kind == 0:
                        act.activation(v_raw[:, hp, :], pv[:, :], ACT.Copy)
                        act.activation(v_sq[:, hp, :], pv[:, :], ACT.Square).then_inc(o_evicted.sem, 1)
                    else:
                        act.activation(v_hi[:, hp, :], pv[:, :], ACT.Copy).then_inc(o_hi_done.sem, 1)

                def head(h, first, last):
                    for u in range(4):
                        w = (u + 1) * P
                        if u == 0:
                            if not first:
                                act.wait_ge(scores_done.sem, scores_done.at(lay, S0 + h * 8))
                            elif kind == 1:
                                act.wait_ge(scores_done.sem, scores_done.at(lay, S0))
                                act.wait_ge(cqk_evicted.sem, cqk_evicted.at(lay, 2 * KC))
                            else:
                                act.wait_ge(u_ready.sem, u_ready.at(lay, KC))
                                act.wait_ge(rope_done.sem, rope_done.at(lay, 2 * KC))
                            act.activation(q_hi[:, :], q_all[:, h, :], ACT.Copy)
                            act.activation(k_hi[:, :], k_all[:, h, :], ACT.Copy).then_inc(qk_hi_done.sem, 1)
                        for comp in range(2):
                            act.wait_ge(neg_ready.sem, neg_ready.at(lay, S0 + h * 8 + (2 * u + comp + 1)))
                            if kind == 0:
                                if u >= 2 or not first:
                                    act.wait_ge(turned.sem, turned.at(lay, h * 4 + (u - 1)))
                                act.activation(prob[:, u % 2, comp, 0:w], sc[comp][:, 0:w], ACT.Exp,
                                               bias=negmax(u % 2, comp), accum_out=rowsum(u % 2, comp))\
                                    .then_inc(exp_done.sem, 1)
                            else:
                                act.activation(prob[:, u % 2, comp, 0:w], prob[:, u % 2, comp, 0:w], ACT.Exp,
                                               bias=negmax(u % 2, comp), scale=-1.0, accum_out=rowsum(u % 2, comp))\
                                    .then_inc(exp_done.sem, 1)
                        if u == 1:
                            if not first:
                                outputs(h - 1)
                            stage_values(h, first)
                        if u or not first:
                            turn_unit(h, u)
                        ahead(lay, c, h, u, last)
                        if u % 2:
                            tanh_gate(lay, branch, h * 2 + u // 2, u // 2)

                def stage_values(h, first):
                    if kind == 0:
                        if first:
                            act.wait_ge(v_evicted.sem, v_evicted.at(lay, TT))
                        act.activation(val_hi[:, 0, :, :], v_all[:, :, head_cols(h)], ACT.Copy)\
                            .then_inc(val_hi_done.sem, 1)
                    else:
                        for comp in range(2):
                            if first and comp == 0:
                                act.wait_ge(v_evicted.sem, v_evicted.at(lay, 2 * TT))
                            o = act.activation(val_hi[:, comp, :, 64 * comp:64 * comp + 64],
                                               v_all[:, :, head_cols(h, comp)], ACT.Copy)
                        o.then_inc(val_hi_done.sem, 1)

                head(0, True, False)
                with act.Fori(1, KC - 1) as h:
                    head(h, False, False)
                head(KC - 1, False, True)
                turn_unit(KC, 0)
                outputs(KC - 1)

            def head_cols(h, comp=None):
                return bass.ds(h * P, P) if comp is None else bass.ds(h * P + 64 * comp, 64)

            def tanh_gate(lay, branch, t, par_):
                act.wait_ge(gate_evicted.sem, gate_evicted.at(lay, branch * KD + t + 1))
                act.activation(tmp[2 + par_][:, :], tmp[par_][:, :], ACT.Tanh,
                               bias=pr[:, bass.ds(PAR_GATE_B + branch * KD + t, 1)], scale=0.5).then_inc(gate_tanh.sem, 1)

            act.wait_ge(par_landed.sem, 16)
            act.wait_ge(consts.sem, N_CONSTS)
            act.wait_ge(lam_prod.sem, 2)
            act.activation(lam_exp, tmp[1][:, 256:256 + 2 * DEPTH], ACT.Exp).then_inc(lam_done.sem, 1)
            act.wait_ge(x_landed.sem, 16)
            act.sem_inc(exp_done.sem, 2)

            with act.Fori(0, DEPTH) as lay:
                for n in range(RING - 1):
                    split_hi(lay, n, n, chunk_cols(n))
                act.wait_ge(par_copied.sem, par_copied.at(lay, 4))
                norm_head(lay, 0, False)
                pairs(lay, C_FFN1_IN, 0, KF, 0)
                act.wait_ge(ext_stored.sem, 16)
                ffn_out_tiles(lay, 0, C_FFN1_OUT)
                norm_tail(lay, 1)
                norm_head(lay, 1, True)
                pairs(lay, C_GLU, KF, KC, 2)
                for i in range(2):
                    for s in range(RING):
                        j = i * RING + s
                        ahead(lay, C_DQK, i, s, i == 1)
                        rope_swap(lay, j, acc[s], ATT_SCALE if i == 0 else 1.0, C_DQK + j)
                values(lay, C_DV)
                conv_norm(lay)
                attention(lay, 0, C_A, 0)
                for i in range(2):
                    for s in range(RING):
                        ahead(lay, C_CQK, i, s, i == 1)
                        if i == 0:
                            if s == 0:
                                diff_norm(lay)
                            act.wait_ge(dn_normed.sem, dn_normed.at(lay, s + 1))
                            act.activation(u_hi[:, s, :], v_raw[:, s, :], ACT.Copy).then_inc(dn_hi.sem, 1)
                values(lay, C_CV)
                attention(lay, 1, C_B, 1)

                def last_branch(i, last):
                    for s in range(RING):
                        ahead(lay, C_C, i, s, last)
                        if s % 2:
                            t = i * 2 + s // 2
                            tanh_gate(lay, 2, t, s // 2)
                            act.wait_ge(mix_added.sem, mix_added.at(lay, KD + t + 1))
                            act.activation(mix_hi[:, t, :], ymix[:, t, :], ACT.Copy, scale=0.5)\
                                .then_inc(mix_hi_done.sem, 1)
                with act.Fori(0, KC - 1) as i:
                    last_branch(i, False)
                last_branch(KC - 1, True)
                for i in range(KD // RING):
                    for s in range(RING):
                        t = i * RING + s
                        ahead(lay, C_WO, i, s, i == KD // RING - 1)
                        y_tile(lay, 1, t, acc[t % 2], C_WO + t + 1, t % 2)
                norm_tail(lay, 3)
                norm_head(lay, 2, True)
                pairs(lay, C_FFN2_IN, KF + KC, KF, 4)
                ffn_out_tiles(lay, 2, C_FFN2_OUT)
                norm_tail(lay, 5)

        @block.vector
        def _(dve):
            def f32(ap):
                return ap.bitcast(F32)

            def par_col(k):
                return pr[:, k:k + 1]

            def sum_squares(lay, g, signal, k):
                for t in range(KD):
                    dve.wait_ge(signal.sem, signal.at(lay, k + t + 1))
                    if t == 0:
                        dve.tensor_copy(sqacc[:, :], tmp[2][:, :]).then_inc(sq_added.sem, 1)
                    else:
                        dve.wait_ge(sq_added.sem, sq_added.at(lay, g * KD + t))
                        dve.tensor_tensor(sqacc[:, :], sqacc[:, :], tmp[2 + t % 2][:, :], ALU.add)\
                            .then_inc(sq_added.sem, 1)

            def diagonal(col, signal):
                for t in range(TT):
                    o = dve.tensor_scalar(diag[:, t, :], ident[:, :], col[:, t:t + 1], None, ALU.mult)
                o.then_inc(signal.sem, 1)

            def norm_scalar(lay, k):
                dve.wait_ge(std_ready.sem, std_ready.at(lay, k + 1))
                dve.reciprocal(rtok, std).then_inc(rtok_ready.sem, 1)
                dve.wait_ge(rtok_ready.sem, rtok_ready.at(lay, k + 1))
                diagonal(rtok, diag_ready)

            def h_low(lay, sub, t):
                g = (0, 2, 4)[sub]
                dve.wait_ge(h_hi_done.sem, h_hi_done.at(lay, sub * KD + t + 1))
                dve.scalar_tensor_tensor(h_lo[:, t, :], x[:, t, :], par_col(g * KD + t), f32(h_hi[:, t, :]),
                                         ALU.mult, ALU.subtract).then_inc(h_ready.sem, 1)

            def residual(lay, sub, follow):
                g = (1, 3, 5)[sub]
                dve.wait_ge(rbc_ready.sem, rbc_ready.at(lay, 2 * sub + 2))
                for t in range(KD + 1):
                    if t < KD:
                        if t >= 2:
                            dve.wait_ge(x_ready.sem, x_ready.at(lay, sub * KD + t - 1))
                        dve.tensor_tensor(tmp[t % 2][:, :], ymix[:, t, :], rbc[:, :], ALU.mult).then_inc(x_scaled.sem, 1)
                    if follow and t >= 2:
                        h_low(lay, sub + 1, t - 2)
                    if t >= 1:
                        dve.wait_ge(x_scaled.sem, x_scaled.at(lay, sub * KD + t))
                        dve.scalar_tensor_tensor(x[:, t - 1, :], tmp[(t - 1) % 2][:, :], par_col(g * KD + t - 1),
                                                 x[:, t - 1, :], ALU.mult, ALU.add).then_inc(x_ready.sem, 1)
                if follow:
                    h_low(lay, sub + 1, KD - 1)
                else:
                    dve.wait_ge(x_ready.sem, x_ready.at(lay, (sub + 1) * KD))

            def ffn_pair(lay, which, c, first_pair, j, b):
                p = first_pair + j
                k = which * KF + j
                dve.wait_ge(rbc_ready.sem, rbc_ready.at(lay, 4 * which + 1))
                dve.wait_ge(chunk_used.sem, chunk_used.at(lay, c + j * 2 + 2))
                dve.tensor_tensor(tmp[0][:, :], acc[b][:, :], rbc[:, :], ALU.mult).then_inc(pair_scaled.sem, 1)
                dve.tensor_tensor(tmp[2][:, :], acc[b + 1][:, :], rbc[:, :], ALU.mult).then_inc(pair_scaled.sem, 1)
                dve.wait_ge(gate_act.sem, gate_act.at(lay, k + (KC if which else 0) + 1))
                dve.wait_ge(pair_scaled.sem, pair_scaled.at(lay, p * 2 + 2))
                dve.tensor_tensor(tmp[3][:, :], tmp[1][:, :], tmp[2][:, :], ALU.mult).then_inc(act_raw.sem, 1)
                dve.wait_ge(act_hi_done.sem, act_hi_done.at(lay, k + 1))
                dve.tensor_tensor(act_lo[:, j, :], tmp[3][:, :], f32(act_hi[:, j, :]), ALU.subtract)\
                    .then_inc(act_ready.sem, 1)

            def ffn(lay, which, c, first_pair):
                with dve.Fori(0, KF // 2) as i:
                    for e in range(2):
                        ffn_pair(lay, which, c, first_pair, i * 2 + e, 2 * e)
                sum_squares(lay, 4 * which + 1, y_evicted, 2 * which * KD)
                norm_scalar(lay, 4 * which + 1)

            def conv_taps(lay, blk):
                i = blk // 2
                taps = range(0, 16) if blk % 2 == 0 else range(16, CONV_K)
                if blk % 2 == 0:
                    dve.wait_ge(z_ready.sem, z_ready.at(lay, i + 1))
                    dve.wait_ge(z_padded.sem, z_padded.at(lay, 1))
                for k in taps:
                    w = par_col(PAR_DW + i * CONV_K + k)
                    to = v_raw[:, i, :] if k % 2 == 0 else conv_odd[:, :]
                    src = z[:, i, k:k + SEQ]
                    if k == 0:
                        o = dve.tensor_scalar(to, src, w, par_col(PAR_CONV_B + i), ALU.mult, ALU.add)
                    elif k == 1:
                        if i:
                            dve.wait_ge(tap_done.sem, tap_done.at(lay, i * (CONV_K + 1)))
                        o = dve.tensor_scalar(to, src, w, None, ALU.mult)
                    else:
                        dve.wait_ge(tap_done.sem, tap_done.at(lay, i * (CONV_K + 1) + k - 1))
                        o = dve.scalar_tensor_tensor(to, src, w, to, ALU.mult, ALU.add)
                    o.then_inc(tap_done.sem, 1)
                if blk % 2:
                    dve.wait_ge(tap_done.sem, tap_done.at(lay, i * (CONV_K + 1) + CONV_K))
                    dve.tensor_tensor(v_raw[:, i, :], v_raw[:, i, :], conv_odd[:, :], ALU.add).then_inc(tap_done.sem, 1)

            def glu(lay):
                dve.memset(z[:, :, 0:ZPAD], 0.0).then_inc(z_padded.sem, 1)
                dve.wait_ge(rbc_ready.sem, rbc_ready.at(lay, 3))
                for j in range(KC):
                    b = 2 * (j % 2)
                    dve.wait_ge(chunk_used.sem, chunk_used.at(lay, C_GLU + 2 * j + 2))
                    if j:
                        dve.wait_ge(z_ready.sem, z_ready.at(lay, j))
                    dve.tensor_tensor(tmp[0][:, :], acc[b + 1][:, :], rbc[:, :], ALU.mult).then_inc(pair_scaled.sem, 1)
                    dve.tensor_tensor(tmp[2][:, :], acc[b][:, :], rbc[:, :], ALU.mult).then_inc(pair_scaled.sem, 1)
                    dve.wait_ge(gate_act.sem, gate_act.at(lay, KF + j + 1))
                    dve.wait_ge(pair_scaled.sem, pair_scaled.at(lay, 2 * (KF + j) + 2))
                    dve.tensor_tensor(z[:, j, ZPAD:ZPAD + SEQ], tmp[1][:, :], tmp[2][:, :], ALU.mult)\
                        .then_inc(z_ready.sem, 1)
                    if j >= 1:
                        conv_taps(lay, j - 1)

            def rope_and_conv(lay):
                dve.wait_ge(tables_landed.sem, tables_landed.at(lay, 32))
                for i in range(2):
                    dve.tensor_tensor(ymix[:, i, :], ymix[:, i, :], rbc[:, :], ALU.mult).then_inc(tables_ready.sem, 1)
                dve.wait_ge(tables_ready.sem, tables_ready.at(lay, 2))
                for j in range(2 * KC):
                    to = (q_all if j < KC else k_all)[:, j % KC, :]
                    dve.wait_ge(swapped.sem, swapped.at(lay, j + 1))
                    dve.scalar_tensor_tensor(to, acc[j % 4][:, :], ATT_SCALE if j < KC else 1.0, ymix[:, 0, :],
                                             ALU.mult, ALU.mult).then_inc(cos_part.sem, 1)
                    dve.tensor_tensor(tmp[j % 2][:, :], tmp[j % 2][:, :], ymix[:, 1, :], ALU.mult).then_inc(sin_part.sem, 1)
                    dve.wait_ge(cos_part.sem, cos_part.at(lay, j + 1))
                    dve.wait_ge(sin_part.sem, sin_part.at(lay, j + 1))
                    dve.tensor_tensor(to, to, tmp[j % 2][:, :], ALU.add).then_inc(rope_done.sem, 1)
                    if j % 2:
                        conv_taps(lay, 3 + j // 2)
                conv_taps(lay, 7)

            def conv_norm(lay):
                dve.wait_ge(ln_sums.sem, ln_sums.at(lay, 1))
                dve.tensor_scalar(rtok2[:, 0:TT], pv[:, 0:TT], 1.0 / C_CONV, None, ALU.mult).then_inc(ln_mean.sem, 1)
                dve.wait_ge(ln_mean.sem, ln_mean.at(lay, 1))
                diagonal(rtok2, ln_diag)
                dve.wait_ge(ln_bcast.sem, ln_bcast.at(lay, 1))
                for t in range(KC):
                    dve.tensor_tensor(v_raw[:, t, :], v_raw[:, t, :], tr[:, :], ALU.subtract).then_inc(ln_centred.sem, 1)
                dve.wait_ge(ln_std.sem, ln_std.at(lay, 1))
                dve.reciprocal(rtok2[:, 0:TT], std2[:, 0:TT]).then_inc(ln_rstd.sem, 1)
                dve.wait_ge(ln_rstd.sem, ln_rstd.at(lay, 1))
                diagonal(rtok2, ln_diag)
                dve.wait_ge(ln_bcast.sem, ln_bcast.at(lay, 2))
                dve.wait_ge(ln_centred.sem, ln_centred.at(lay, KC))
                for t in range(KC):
                    dve.tensor_tensor(v_raw[:, t, :], v_raw[:, t, :], tr[:, :], ALU.mult).then_inc(ln_normed.sem, 1)
                for t in range(KC):
                    dve.wait_ge(conv_hi.sem, conv_hi.at(lay, t + 1))
                    dve.tensor_tensor(u_lo[:, t, :], v_sq[:, t, :], f32(u_hi[:, t, :]), ALU.subtract)\
                        .then_inc(u_ready.sem, 1)

            def diff_norm_scalars(lay):
                dve.wait_ge(dn_std.sem, dn_std.at(lay, 1))
                dve.reciprocal(rtok2, std2).then_inc(dn_rtok.sem, 1)
                dve.wait_ge(dn_rtok.sem, dn_rtok.at(lay, 1))
                dve.tensor_scalar(rtok2, rtok2, out_scale[:, bass.ds(lay, 1)], None, ALU.mult).then_inc(dn_rtok.sem, 1)
                dve.wait_ge(dn_rtok.sem, dn_rtok.at(lay, 2))

            def diff_norm(lay, h):
                diagonal(rtok2[:, 4 * h:4 * h + 4], dn_diag)
                dve.wait_ge(dn_bcast.sem, dn_bcast.at(lay, h + 1))
                dve.tensor_tensor(v_raw[:, h, :], v_raw[:, h, :], tr[:, :], ALU.mult).then_inc(dn_normed.sem, 1)
                dve.wait_ge(dn_hi.sem, dn_hi.at(lay, h + 1))
                dve.tensor_tensor(u_lo[:, h, :], v_raw[:, h, :], f32(u_hi[:, h, :]), ALU.subtract)\
                    .then_inc(u_ready.sem, 1)

            def chunk_qk(lay):
                diff_norm_scalars(lay)
                for j in range(2 * KC):
                    if j < KC:
                        diff_norm(lay, j)
                    to = (q_all if j < KC else k_all)[:, j % KC, :]
                    dve.wait_ge(chunk_used.sem, chunk_used.at(lay, C_CQK + j + 1))
                    dve.scalar_tensor_tensor(to, acc[j % 4][:, :], ATT_SCALE if j < KC else 1.0, rbc[:, :],
                                             ALU.mult, ALU.mult).then_inc(cqk_evicted.sem, 1)

            def gate_out(lay, branch, t, b, c):
                k = branch * KD + t
                dve.wait_ge(chunk_used.sem, chunk_used.at(lay, c + t * 2 + 1))
                if branch == 1 and not (isinstance(t, int) and t < 2):
                    dve.wait_ge(mix_added.sem, mix_added.at(lay, t - 1))
                elif branch == 2:
                    dve.wait_ge(mix_added.sem, mix_added.at(lay, t + (KD - 1)))
                dve.tensor_tensor(tmp[b][:, :], acc[b][:, :], rbc[:, :], ALU.mult).then_inc(gate_evicted.sem, 1)
                dve.wait_ge(gate_tanh.sem, gate_tanh.at(lay, k + 1))
                dve.wait_ge(chunk_used.sem, chunk_used.at(lay, c + t * 2 + 2))
                if branch == 0:
                    dve.scalar_tensor_tensor(ymix[:, t, :], tmp[2 + b][:, :], 1.0, acc[2 + b][:, :], ALU.add, ALU.mult)\
                        .then_inc(out_evicted.sem, 1)
                    return
                dve.scalar_tensor_tensor(tmp[b][:, :], tmp[2 + b][:, :], 1.0, acc[2 + b][:, :], ALU.add, ALU.mult)\
                    .then_inc(out_evicted.sem, 1)
                dve.wait_ge(out_evicted.sem, out_evicted.at(lay, k + 1))
                dve.tensor_tensor(ymix[:, t, :], ymix[:, t, :], tmp[b][:, :], ALU.add).then_inc(mix_added.sem, 1)

            def attention(lay, kind, c, branch):
                U0, H0, S0, T0 = 16 * kind, KC * kind, 32 * kind, 16 * kind
                n_comp = 1 + kind

                def turn_unit(h, u):
                    hp, up = (h, u - 1) if u else (h - 1, 3)
                    w = (up + 1) * P
                    for comp in range(n_comp):
                        m = (hp * 4 + up) * n_comp + (T0 + comp)
                        dve.wait_ge(pt_hi_done.sem, pt_hi_done.at(lay, m + 1))
                        dve.tensor_tensor(pt_lo[:, comp, 0:up + 1, :].rearrange("p a b -> p (a b)"), tr[:, 0:w],
                                          f32(pt_hi[:, comp, 0:up + 1, :]).rearrange("p a b -> p (a b)"), ALU.subtract)\
                            .then_inc(pt_ready.sem, 1)

                def outputs(hp):
                    dve.wait_ge(o_hi_done.sem, o_hi_done.at(lay, hp + 1))
                    dve.tensor_tensor(v_lo[:, hp, :], pv[:, :], f32(v_hi[:, hp, :]), ALU.subtract)\
                        .then_inc(o_evicted.sem, 1)

                def stage_values(h):
                    dve.wait_ge(val_hi_done.sem, val_hi_done.at(lay, h + (H0 + 1)))
                    if kind == 0:
                        dve.tensor_tensor(val_lo[:, 0, :, :], v_all[:, :, bass.ds(h * P, P)], f32(val_hi[:, 0, :, :]),
                                          ALU.subtract).then_inc(val_staged.sem, 1)
                        return
                    for comp in range(2):
                        to = slice(64 * comp, 64 * comp + 64)
                        o = dve.tensor_tensor(val_lo[:, comp, :, to], v_all[:, :, bass.ds(h * P + 64 * comp, 64)],
                                              f32(val_hi[:, comp, :, to]), ALU.subtract)
                    o.then_inc(val_staged.sem, 1)

                def head(h, first):
                    for u in range(4):
                        w = (u + 1) * P
                        even = u % 2
                        if u == 0:
                            dve.wait_ge(qk_hi_done.sem, qk_hi_done.at(lay, h + (H0 + 1)))
                            dve.tensor_tensor(q_lo[:, :], q_all[:, h, :], f32(q_hi[:, :]), ALU.subtract)
                            dve.tensor_tensor(k_lo[:, :], k_all[:, h, :], f32(k_hi[:, :]), ALU.subtract)\
                                .then_inc(qk_staged.sem, 1)
                            if kind == 1:
                                dve.wait_ge(strip_landed.sem, strip_landed.at(lay, h * 16 + 16))
                        for comp in range(2):
                            dve.wait_ge(scores_done.sem, scores_done.at(lay, h * 8 + (S0 + 2 * u + comp + 1)))
                            if kind == 0:
                                dve.tensor_reduce(negmax(even, comp), sc[comp][:, 0:w], AX.X, ALU.max, negate=True)\
                                    .then_inc(neg_ready.sem, 1)
                            else:
                                if comp == 0:
                                    dve.wait_ge(turned.sem, turned.at(lay, 16 if first and u < 2 else (h * 8 + (16 + 2 * u - 2))))
                                dve.memset(rowsum(even, comp), 0.0)
                                dve.tensor_tensor_reduce(prob[:, even, comp, 0:w], sc[comp][:, 0:w],
                                                         strip[:, comp, SEQ - w:SEQ], -1.0, 3.0e38, ALU.add, ALU.min,
                                                         negmax(even, comp)).then_inc(neg_ready.sem, 1)
                        if u == 1:
                            if not first and kind == 1:
                                outputs(h - 1)
                            stage_values(h)
                        if u or not first:
                            turn_unit(h, u)
                        dve.wait_ge(exp_done.sem, exp_done.at(lay, h * 8 + (S0 + 2 * u + 2)))
                        steps = (h * 12 + 3 * u) if kind == 0 else (h * 4 + (48 + u))
                        if kind or u or not first:
                            dve.wait_ge(prob_ready.sem, prob_ready.at(lay, h * 4 + (U0 + u)))
                        dve.reciprocal(rinv, small[:, 44 + 2 * even:46 + 2 * even]).then_inc(row_steps.sem, 1)
                        dve.wait_ge(row_steps.sem, row_steps.at(lay, steps + 1))
                        if kind == 0:
                            dve.tensor_scalar(lam_r1, rinv[:, 1:2], neg_lam[:, bass.ds(lay, 1)], None, ALU.mult)\
                                .then_inc(row_steps.sem, 1)
                            dve.tensor_scalar(prob[:, even, 0, 0:w], prob[:, even, 0, 0:w], rinv[:, 0:1], None, ALU.mult)\
                                .then_inc(row_steps.sem, 1)
                            dve.wait_ge(row_steps.sem, row_steps.at(lay, steps + 3))
                            dve.scalar_tensor_tensor(prob[:, even, 0, 0:w], prob[:, even, 1, 0:w], lam_r1,
                                                     prob[:, even, 0, 0:w], ALU.mult, ALU.add).then_inc(prob_ready.sem, 1)
                        else:
                            for comp in range(2):
                                o = dve.tensor_scalar(prob[:, even, comp, 0:w], prob[:, even, comp, 0:w],
                                                      rinv[:, comp:comp + 1], None, ALU.mult)
                            o.then_inc(prob_ready.sem, 1)
                        if u % 2:
                            gate_out(lay, branch, h * 2 + u // 2, u // 2, c)

                if kind == 1:
                    dve.wait_ge(pv_done.sem, pv_done.at(lay, 16))
                    for v in (val_hi, val_lo):
                        f = f32(v[:, :, :, :])
                        dve.memset(f[:, 0, :, 64:P], 0.0)
                        o = dve.memset(f[:, 1, :, 0:64], 0.0)
                    o.then_inc(val_zeroed.sem, 1)
                head(0, True)
                with dve.Fori(1, KC) as h:
                    head(h, False)
                turn_unit(KC, 0)
                if kind == 1:
                    outputs(KC - 1)

            dve.wait_ge(zeroed.sem, 3)
            for r in (0, 64):
                dve.memset(mask_q[r:r + 1, 0:64].bitcast(F32), 1.0).then_inc(consts.sem, 1)
                dve.memset(mask_k[r:r + 1, :].bitcast(F32), NEG_R).then_inc(consts.sem, 1)
            dve.wait_ge(lam_landed.sem, 16)
            lam = tmp[0][:, :].rearrange("p (l a b d) -> p l a b d", l=DEPTH, a=2, b=2)
            for l in range(DEPTH):
                for a in range(2):
                    o = dve.tensor_tensor(tmp[1][:, (2 * l + a) * 64:(2 * l + a) * 64 + 64], lam[:, l, a, 0, :],
                                          lam[:, l, a, 1, :], ALU.mult)
            o.then_inc(lam_prod.sem, 1)
            dve.wait_ge(lam_prod.sem, 1)
            dve.tensor_reduce(tmp[1][:, 256:256 + 2 * DEPTH], tmp[1][:, 0:256].rearrange("p (n d) -> p n d", d=64),
                              AX.X, ALU.add).then_inc(lam_prod.sem, 1)
            rel = ymix[0:DEPTH * HEADS_CHUNK, 0:2, :].rearrange("p a b -> p (a b)")
            dve.wait_ge(rel_landed.sem, 16)
            dve.memset(rel[:, EXT_LEFT + N_REL:EXT], 0.0).then_inc(rel_ready.sem, 1)
            dve.tensor_copy(rel[:, 0:EXT_LEFT], rel[:, EXT_LEFT:EXT_LEFT + 1].to_broadcast([DEPTH * HEADS_CHUNK, EXT_LEFT]))\
                .then_inc(rel_ready.sem, 1)
            dve.wait_ge(lam_done.sem, 1)
            for l in range(DEPTH):
                dve.tensor_scalar(neg_lam[:, l:l + 1], lam_exp[:, 2 * l + 1:2 * l + 2], lam_exp[:, 2 * l:2 * l + 1],
                                  -lam_init(l), ALU.subtract, ALU.add).then_inc(setup.sem, 1)
            dve.wait_ge(setup.sem, DEPTH)
            dve.wait_ge(par_landed.sem, 16)
            dve.wait_ge(x_landed.sem, 16)
            dve.wait_ge(consts.sem, N_CONSTS)
            for s, k in ((pair_scaled, 4), (y_evicted, 2), (pt_ready, 1), (o_evicted, 1), (gate_evicted, 2), (out_evicted, 2)):
                dve.sem_inc(s.sem, k)

            with dve.Fori(0, DEPTH) as lay:
                dve.tensor_copy(pr[:, :], par_all[:, lay, :]).then_inc(par_copied.sem, 1)
                dve.wait_ge(par_copied.sem, par_copied.at(lay, 1))
                for k, n in ((KD, KD), (5 * KD, KD), (PAR_GATE_B, 3 * KD)):
                    dve.tensor_scalar(pr[:, k:k + n], pr[:, k:k + n], 0.5, None, ALU.mult).then_inc(par_copied.sem, 1)
                dve.wait_ge(par_copied.sem, par_copied.at(lay, 4))
                for t in range(KD):
                    h_low(lay, 0, t)
                sum_squares(lay, 0, squared, 0)
                norm_scalar(lay, 0)
                ffn(lay, 0, C_FFN1_IN, 0)
                residual(lay, 0, True)
                sum_squares(lay, 2, squared, KD)
                norm_scalar(lay, 2)
                glu(lay)
                rope_and_conv(lay)
                conv_norm(lay)
                attention(lay, 0, C_A, 0)
                chunk_qk(lay)
                attention(lay, 1, C_B, 1)

                def last_branch(t, b):
                    gate_out(lay, 2, t, b, C_C)
                    dve.wait_ge(mix_hi_done.sem, mix_hi_done.at(lay, t + 1))
                    dve.scalar_tensor_tensor(mix_lo[:, t, :], ymix[:, t, :], 0.5, f32(mix_hi[:, t, :]),
                                             ALU.mult, ALU.subtract).then_inc(mix_ready.sem, 1)
                with dve.Fori(0, KD // 2) as i:
                    for e in range(2):
                        last_branch(i * 2 + e, e)
                sum_squares(lay, 3, y_evicted, KD)
                norm_scalar(lay, 3)
                residual(lay, 1, True)
                sum_squares(lay, 4, squared, 2 * KD)
                norm_scalar(lay, 4)
                ffn(lay, 1, C_FFN2_IN, KF + KC)
                residual(lay, 2, False)

        @block.tensor
        def _(pe):
            def products(slot, kk, stat_cols, xh, xl, out, start, stop):
                a = kk * P
                whi, wlo = w_hi[:, slot, a:a + P], w_lo[:, slot, a:a + P]
                pe.matmul(out, whi, xh, start=start, stop=False)
                pe.matmul(out, whi, xl, start=False, stop=False)
                return pe.matmul(out, wlo, xh, start=False, stop=stop)

            def split(lay, n):
                pe.wait_ge(split_done.sem, split_done.at(lay, n + 1))

            def chunk(lay, n, slot, k0, n_k, hi, lo, out, start, stop):
                split(lay, n)
                for kk in range(n_k):
                    o = products(slot, kk, P, hi[:, k0 + kk, :], lo[:, k0 + kk, :], out[:, :],
                                 start and kk == 0, stop and kk == n_k - 1)
                o.then_inc(chunk_used.sem, 1)

            def column_sums(src, signal, tiles, col):
                for t in range(TT):
                    for i in range(tiles):
                        o = pe.matmul(pv[:, col + t:col + t + 1], src(i)[:, t * P:(t + 1) * P], ones[:, 0:1],
                                      start=(i == 0), stop=(i == tiles - 1))
                if signal is not None:
                    o.then_inc(signal.sem, 1)

            def spread(signal):
                pe.matmul(tr[:, :], ones[:, :], diag[:, :, :].rearrange("p a b -> p (a b)"), start=True, stop=True)\
                    .then_inc(signal.sem, 1)

            def norm_sums(lay, k):
                pe.wait_ge(sq_added.sem, sq_added.at(lay, (k + 1) * KD))
                column_sums(lambda i: sqacc, summed, 1, 0)

            def norm_spread(lay, k):
                pe.wait_ge(diag_ready.sem, diag_ready.at(lay, k + 1))
                spread(bcast)

            def pairs(lay, c, first_pair, n_pairs, sub):
                def pair(i, e, j, head, tail):
                    b = 2 * e
                    pe.wait_ge(pair_scaled.sem, pair_scaled.at(lay, (first_pair + j) * 2 - 2))
                    split(lay, c + j * 2 + 1)
                    for k in range(KD):
                        if head:
                            pe.wait_ge(h_ready.sem, h_ready.at(lay, sub * KD + k + 1))
                        for half in range(2):
                            o = products(2 * e + half, k, P, h_hi[:, k, :], h_lo[:, k, :], acc[b + half][:, :],
                                         k == 0, k == KD - 1)
                            if k == KD - 1:
                                o.then_inc(chunk_used.sem, 1)
                        if tail and k == 3:
                            norm_sums(lay, 2 * sub)
                        if tail and k == 6:
                            norm_spread(lay, 2 * sub)
                pair(0, 0, 0, True, False)
                pair(0, 1, 1, False, True)
                with pe.Fori(1, n_pairs // 2) as i:
                    for e in range(2):
                        pair(i, e, i * 2 + e, False, False)

            def ffn_out_tiles(lay, sub, which, c, last_pair):
                def tile(t, e):
                    pe.wait_ge(pair_scaled.sem, pair_scaled.at(lay, last_pair * 2))
                    pe.wait_ge(y_evicted.sem, y_evicted.at(lay, sub * KD + t - 1))
                    for s, n_k in enumerate(FFN_OUT_K):
                        pe.wait_ge(act_ready.sem, act_ready.at(lay, which * KF + FFN_OUT_AT[s + 1]))
                        chunk(lay, c + t * RING + s, s, FFN_OUT_AT[s], n_k, act_hi, act_lo, acc[e], s == 0, s == RING - 1)
                with pe.Fori(0, KD // 2) as i:
                    for e in range(2):
                        tile(i * 2 + e, e)
                norm_sums(lay, 2 * sub + 1)
                norm_spread(lay, 2 * sub + 1)

            def values(lay, c):
                for m in range(TT):
                    split(lay, c + m)
                    for kk in range(2):
                        k = 2 * m + kk
                        for t in range(TT):
                            whi = w_hi[:, m, kk * SEQ:(kk + 1) * SEQ]
                            wlo = w_lo[:, m, kk * SEQ:(kk + 1) * SEQ]
                            hh, hl = h_hi[:, k, t * P:(t + 1) * P], h_lo[:, k, t * P:(t + 1) * P]
                            pe.matmul(acc[t][:, :], hh, whi, start=(k == 0), stop=False)
                            pe.matmul(acc[t][:, :], hh, wlo, start=False, stop=False)
                            o = pe.matmul(acc[t][:, :], hl, whi, start=False, stop=(k == KD - 1))
                    o.then_inc(chunk_used.sem, 1)

            def attention(lay, kind, c, branch, out_hi, out_lo):
                U0, H0, S0, T0 = 16 * kind, KC * kind, 32 * kind, 16 * kind
                n_comp = 1 + kind

                def scores(h, u):
                    w = (u + 1) * P
                    if u == 0:
                        pe.wait_ge(qk_staged.sem, qk_staged.at(lay, h + (H0 + 1)))
                    for comp in range(2):
                        r = slice(64 * comp, 64 * comp + 64)
                        pe.wait_ge(exp_done.sem, exp_done.at(lay, h * 8 + (S0 + 2 * u + comp - 1)))
                        qh, ql = q_hi[r, u * P:w], q_lo[r, u * P:w]
                        out = sc[comp][:, 0:w]
                        pe.matmul(out, qh, k_hi[r, 0:w], start=True, stop=False)
                        pe.matmul(out, qh, k_lo[r, 0:w], start=False, stop=False)
                        pe.matmul(out, ql, k_hi[r, 0:w], start=False, stop=False)
                        pe.matmul(sc[comp][:, w - 64:w], mask_q[r, :], mask_k[r, :], start=False, stop=True)\
                            .then_inc(scores_done.sem, 1)

                def turn(h, u, comp):
                    hp, up = (h, u - 1) if u else (h - 1, 3)
                    m = (hp * 4 + up) * n_comp + (T0 + comp)
                    pe.wait_ge(prob_ready.sem, prob_ready.at(lay, hp * 4 + (U0 + up + 1)))
                    pe.wait_ge(pt_ready.sem, pt_ready.at(lay, m))
                    for j in range(up + 1):
                        o = pe.transpose(tr[:, j * P:(j + 1) * P], prob[:, up % 2, comp, j * P:(j + 1) * P], ident[:, :])
                    o.then_inc(turned.sem, 1)

                def weigh(h, u):
                    hp, up = (h, u - 2) if u >= 2 else (h - 1, u + 2)
                    m = (hp * 4 + up) * n_comp + (T0 + n_comp)
                    if up == 0:
                        pe.wait_ge(val_staged.sem, val_staged.at(lay, hp + (H0 + 1)))
                        pe.wait_ge(o_evicted.sem, o_evicted.at(lay, hp + H0))
                        if kind == 1:
                            pe.wait_ge(val_zeroed.sem, val_zeroed.at(lay, 1))
                    pe.wait_ge(pt_ready.sem, pt_ready.at(lay, m))
                    n = n_comp * (up + 1) * 3
                    i = 0
                    for comp in range(n_comp):
                        for j in range(up + 1):
                            for a, b in ((val_hi, pt_hi), (val_hi, pt_lo), (val_lo, pt_hi)):
                                o = pe.matmul(pv[:, up * P:(up + 1) * P], a[:, comp, j, :], b[:, comp, j, :],
                                              start=(i == 0), stop=(i == n - 1))
                                i += 1
                    o.then_inc(pv_done.sem, 1)

                def dense(h, u, part):
                    t = h * 2 + u // 2
                    e = u // 2
                    n = c + t * 2
                    if u % 2 == 0 and part == 0:
                        pe.wait_ge(gate_evicted.sem, gate_evicted.at(lay, branch * KD + t - 1))
                        split(lay, n)
                    if u % 2 == 1 and part == 1:
                        pe.wait_ge(out_evicted.sem, out_evicted.at(lay, branch * KD + t - 1))
                        split(lay, n + 1)
                        pe.wait_ge(u_ready.sem, u_ready.at(lay, KC * (branch + 1)))
                    if u % 2 == 0:
                        ks = range(0, 3) if part == 0 else range(3, 6)
                    else:
                        ks = range(6, 8) if part == 0 else ()
                    for k in ks:
                        o = products(2 * e, k, P, h_hi[:, k, :], h_lo[:, k, :], acc[e][:, :], k == 0, k == KD - 1)
                        if k == KD - 1:
                            o.then_inc(chunk_used.sem, 1)
                    if u % 2 == 1 and part == 1:
                        for k in range(KC):
                            o = products(2 * e + 1, k, P, out_hi[:, k, :], out_lo[:, k, :], acc[2 + e][:, :],
                                         k == 0, k == KC - 1)
                        o.then_inc(chunk_used.sem, 1)

                def head(h, first):
                    for u in range(4):
                        scores(h, u)
                        if u >= 2 or not first:
                            weigh(h, u)
                        if u or not first:
                            turn(h, u, 0)
                        dense(h, u, 0)
                        if kind == 1 and (u or not first):
                            turn(h, u, 1)
                        dense(h, u, 1)

                pe.wait_ge(v_evicted.sem, v_evicted.at(lay, TT * (kind + 1)))
                head(0, True)
                with pe.Fori(1, KC) as h:
                    head(h, False)
                weigh(KC, 0)
                turn(KC, 0, 0)
                if kind == 1:
                    turn(KC, 0, 1)
                weigh(KC, 1)

            pe.wait_ge(consts.sem, N_CONSTS)
            for s, k in ((chunk_used, RING), (pv_done, 1)):
                pe.sem_inc(s.sem, k)

            with pe.Fori(0, DEPTH) as lay:
                pairs(lay, C_FFN1_IN, 0, KF, 0)
                ffn_out_tiles(lay, 0, 0, C_FFN1_OUT, KF - 1)
                pairs(lay, C_GLU, KF, KC, 1)
                pe.wait_ge(pair_scaled.sem, pair_scaled.at(lay, 2 * (KF + KC)))
                for j in range(2 * KC):
                    if j >= 4:
                        pe.wait_ge(cos_part.sem, cos_part.at(lay, j - 3))
                    chunk(lay, C_DQK + j, j % RING, 0, KD, h_hi, h_lo, acc[j % 4], True, True)
                pe.wait_ge(cos_part.sem, cos_part.at(lay, 2 * KC))
                values(lay, C_DV)
                pe.wait_ge(tap_done.sem, tap_done.at(lay, KC * (CONV_K + 1)))
                column_sums(lambda i: v_raw[:, i, :], ln_sums, KC, 0)
                pe.wait_ge(ln_diag.sem, ln_diag.at(lay, 1))
                spread(ln_bcast)
                pe.wait_ge(ln_squared.sem, ln_squared.at(lay, KC))
                column_sums(lambda i: v_sq[:, i, :], ln_sums, KC, 0)
                pe.wait_ge(ln_diag.sem, ln_diag.at(lay, 2))
                spread(ln_bcast)
                attention(lay, 0, C_A, 0, u_hi, u_lo)
                pe.wait_ge(o_evicted.sem, o_evicted.at(lay, KC))
                for h in range(KC):
                    column_sums(lambda i: v_sq[:, h, :], dn_sums if h == KC - 1 else None, 1, 4 * h)
                pe.wait_ge(out_evicted.sem, out_evicted.at(lay, KD))
                for j in range(2 * KC):
                    if j >= 4:
                        pe.wait_ge(cqk_evicted.sem, cqk_evicted.at(lay, j - 3))
                    chunk(lay, C_CQK + j, j % RING, 0, KD, h_hi, h_lo, acc[j % 4], True, True)
                    if j < KC:
                        pe.wait_ge(dn_diag.sem, dn_diag.at(lay, j + 1))
                        spread(dn_bcast)
                pe.wait_ge(cqk_evicted.sem, cqk_evicted.at(lay, 2 * KC))
                values(lay, C_CV)
                attention(lay, 1, C_B, 1, u_hi, u_lo)
                with pe.Fori(0, KD // 2) as i:
                    for e in range(2):
                        t = i * 2 + e
                        pe.wait_ge(o_evicted.sem, o_evicted.at(lay, 2 * KC))
                        pe.wait_ge(gate_evicted.sem, gate_evicted.at(lay, t + (2 * KD - 1)))
                        chunk(lay, C_C + t * 2, 2 * e, 0, KD, h_hi, h_lo, acc[e], True, True)
                        pe.wait_ge(out_evicted.sem, out_evicted.at(lay, t + (2 * KD - 1)))
                        chunk(lay, C_C + t * 2 + 1, 2 * e + 1, 0, KC, v_hi, v_lo, acc[2 + e], True, True)
                pe.wait_ge(gate_evicted.sem, gate_evicted.at(lay, 3 * KD))
                for t in range(KD):
                    pe.wait_ge(y_evicted.sem, y_evicted.at(lay, KD + t - 1))
                    split(lay, C_WO + t)
                    for k in range(KD):
                        if t == 0:
                            pe.wait_ge(mix_ready.sem, mix_ready.at(lay, k + 1))
                        o = products(t % RING, k, P, mix_hi[:, k, :], mix_lo[:, k, :], acc[t % 2][:, :], k == 0, k == KD - 1)
                    o.then_inc(chunk_used.sem, 1)
                norm_sums(lay, 3)
                norm_spread(lay, 3)
                pairs(lay, C_FFN2_IN, KF + KC, KF, 2)
                ffn_out_tiles(lay, 2, 1, C_FFN2_OUT, 2 * KF + KC - 1)


def tiles(w, n_k):
    k, n = w.shape
    return w.reshape(n_k, P, n // P, P).transpose(2, 1, 0, 3).reshape(n // P, P, n_k * P)


def kernel(x, norm_g, ffn1_in, ffn1_out, w_in, gate_b, conv_dw, conv_b, conv_ln, w_conv_out, diff_lambda,
           w_diff_out, rel_bias, w_chunk_out, w_o, ffn2_in, ffn2_out):
    import concourse.bacc as _bacc
    from concourse.bass_utils import run_bass_kernel_spmd as _run

    a = {k: np.asarray(v) for k, v in dict(
        x=x, norm_g=norm_g, ffn1_in=ffn1_in, ffn1_out=ffn1_out, w_in=w_in, gate_b=gate_b, conv_dw=conv_dw,
        conv_b=conv_b, conv_ln=conv_ln, w_conv_out=w_conv_out, diff_lambda=diff_lambda, w_diff_out=w_diff_out,
        rel_bias=rel_bias, w_chunk_out=w_chunk_out, w_o=w_o, ffn2_in=ffn2_in, ffn2_out=ffn2_out).items()}

    ffn_in_t, ffn_out_t, mix_t, br_t, wo_t, par_t = [], [], [], [], [], []
    for l in range(DEPTH):
        for f in ("ffn1", "ffn2"):
            t = tiles(a[f + "_in"][l], KD)
            ffn_in_t.append(np.stack([t[:KF], t[KF:]], axis=1).reshape(2 * KF, P, CHUNK))
            ffn_out_t.append(tiles(a[f + "_out"][l], KF))
        t = tiles(a["w_in"][l], KD)
        o_glu, o_dq, o_dk, o_dv, o_cq, o_ck, o_cv, o_gate = 0, 8, 12, 16, 20, 24, 28, 32

        def value_chunks(o):
            w = a["w_in"][l][:, o * P:o * P + SEQ]
            return w.reshape(TT, 2, P, SEQ).transpose(0, 2, 1, 3).reshape(TT, P, CHUNK)

        glu = np.stack([t[o_glu:o_glu + KC], t[o_glu + KC:o_dq]], axis=1).reshape(2 * KC, P, CHUNK)
        mix_t.append(np.concatenate([
            glu, t[o_dq:o_dv], value_chunks(o_dv), t[o_gate:o_gate + KD],
            t[o_cq:o_cv], value_chunks(o_cv), t[o_gate + KD:o_gate + 3 * KD]]))
        br_t.append(np.concatenate([tiles(a[n][l], KC) for n in ("w_conv_out", "w_diff_out", "w_chunk_out")]))
        wo_t.append(tiles(a["w_o"][l], KD))
        cols = [a["norm_g"][l].reshape(6 * KD, P), a["gate_b"][l].reshape(3 * KD, P),
                a["conv_dw"][l].reshape(CONV_K, KC, P).transpose(1, 0, 2).reshape(KC * CONV_K, P),
                a["conv_b"][l].reshape(KC, P), a["conv_ln"][l].reshape(2 * KC, P)]
        par_t.append(np.concatenate(cols).T)

    inv = (np.float32(10000.0) ** (-np.arange(0, 64, 2, dtype=np.float32) / np.float32(64))).astype(np.float32)
    ang = np.arange(SEQ, dtype=np.float32)[:, None] * inv[None, :]
    cos, sin = np.cos(ang).T.astype(np.float32), np.sin(ang).T.astype(np.float32)
    rope = np.stack([np.concatenate([cos] * 4), np.concatenate([-sin, sin] * 2)])

    arrays = {
        "xT": a["x"][0].T.reshape(KD, P, SEQ).transpose(1, 0, 2),
        "ffn_in": np.concatenate(ffn_in_t), "ffn_out": np.concatenate(ffn_out_t),
        "mix_in": np.concatenate(mix_t), "br_out": np.concatenate(br_t), "wo": np.concatenate(wo_t),
        "par": np.stack(par_t, axis=1),
        "lamb": a["diff_lambda"].reshape(DEPTH * 4 * 64),
        "relb": a["rel_bias"][:, :, ::-1].reshape(DEPTH * HEADS_CHUNK, N_REL),
        "rope": rope,
    }
    arrays = {k: np.ascontiguousarray(v) for k, v in arrays.items()}
    nc = _bacc.Bacc("TRN2", target_bir_lowering=False, num_devices=1, dynamic_dma_scratch_size=1024)
    args = [nc.dram_tensor(k, v.shape, mybir.dt.from_np(v.dtype), kind="ExternalInput").ap() for k, v in arrays.items()]
    args.append(nc.dram_tensor("outT", (P, KD, SEQ), F32, kind="ExternalOutput").ap())
    build(nc, *args)
    r = _run(nc, [arrays], core_ids=[0])
    out = np.asarray(r.results[0]["outT"])
    return np.ascontiguousarray(out.transpose(1, 0, 2).reshape(D_MODEL, SEQ).T).reshape(1, SEQ, D_MODEL)
```

```python
import math
from contextlib import ExitStack

import numpy as np

import concourse.bass as bass
from concourse import mybir

ACT = mybir.ActivationFunctionType
ALU = mybir.AluOpType
AX = mybir.AxisListType
F32 = mybir.dt.float32
F32R = mybir.dt.float32r

P = 128
D_MODEL = 1024
SEQ = 512
DEPTH = 2
D_FF = 2816
C_CONV = 512
CONV_K = 31
EPS = 1e-6
N_REL = 320
HEADS_CHUNK = 8
ATT_SCALE = 64 ** -0.5

KD = D_MODEL // P
KF = D_FF // P
KC = C_CONV // P
TT = SEQ // P
RING = 4
CHUNK = KD * P
FFN_OUT_K = (6, 6, 5, 5)
FFN_OUT_AT = (0, 6, 12, 17, 22)

C_FFN1_IN = 0
C_FFN1_OUT = C_FFN1_IN + 2 * KF
C_GLU = C_FFN1_OUT + 4 * KD
C_DQK = C_GLU + 2 * KC
C_DV = C_DQK + 2 * KC
C_A = C_DV + 4
C_CQK = C_A + 2 * KD
C_CV = C_CQK + 2 * KC
C_B = C_CV + 4
C_C = C_B + 2 * KD
C_WO = C_C + 2 * KD
C_FFN2_IN = C_WO + KD
C_FFN2_OUT = C_FFN2_IN + 2 * KF
CHUNKS = C_FFN2_OUT + 4 * KD
assert CHUNKS == 240 and all(c % RING == 0 for c in (C_FFN1_OUT, C_GLU, C_DQK, C_DV, C_A, C_CQK, C_CV, C_B, C_C, C_WO, C_FFN2_IN, C_FFN2_OUT))


def chunk_cols(n):
    if C_FFN1_OUT <= n < C_GLU or C_FFN2_OUT <= n < CHUNKS:
        return FFN_OUT_K[n % RING] * P
    if C_A <= n < C_CQK:
        return KC * P
    if C_C <= n < C_WO:
        return KD * P if n % 2 == 0 else KC * P
    return KD * P


PAR_NORM = 0
PAR_GATE_B = PAR_NORM + 6 * KD
PAR_DW = PAR_GATE_B + 3 * KD
PAR_CONV_B = PAR_DW + KC * CONV_K
PAR_LN = PAR_CONV_B + KC
N_PAR = PAR_LN + 2 * KC

PHASES = (C_FFN1_IN, C_FFN1_OUT, C_GLU, C_A, C_CQK, C_C, C_WO, C_FFN2_IN, C_FFN2_OUT, CHUNKS)
AFTER_NORM = (C_GLU, C_FFN2_IN)
N_CONSTS = 3 + DEPTH + 4
HALVES = (range(0, 16), range(16, CONV_K))
ROPE_TAPS = [range(k, k + 3) for k in range(HALVES[0][-1] + 1, CONV_K, 3)]
FIRST_TAPS = (range(0, 2), range(2, 7), range(7, 11), range(11, 15))
HEAD_TAPS = (CONV_K - FIRST_TAPS[-1][-1] - 1) // 2
LATER_TAPS = (range(0, 3), range(3, 6), range(6, HEAD_TAPS))
NEG_R = -2.0 ** 100


def lam_init(l):
    return 0.8 - 0.6 * math.exp(-0.3 * l)


EXT_LEFT = 256
EXT = EXT_LEFT + N_REL + 64


class Signal:

    def __init__(self, sem, per_layer, credit=0):
        self.sem, self.per_layer, self.credit = sem, per_layer, credit

    def at(self, lay, k):
        return lay * self.per_layer + (k + self.credit)


def build(nc, xT, ffn_in, ffn_out, mix_in, out_ab, out_c, wo, par, lamb, relb, rope, outT):
    with ExitStack() as ctx:
        def sb(name, shape, dt=F32):
            return ctx.enter_context(nc.sbuf_tensor(name, shape, dt))

        def bank(name):
            return ctx.enter_context(nc.psum_tensor(name, [P, SEQ], F32))

        def sig(name, per_layer, credit=0):
            return Signal(ctx.enter_context(nc.semaphore(name)), per_layer, credit)

        region_at = (nc.sbuf_base + 31) // 32 * 32
        region = sb("region", [P, 2 * KF * SEQ])

        def at(name, offset, shape, dt=F32):
            return nc.alloc_sbuf_tensor_at(name, [P, *shape], dt, offset=region_at + offset)

        TILE = 4 * SEQ
        act_hi = at("act_hi", 0, [KF, SEQ], F32R)
        act_lo = at("act_lo", KF * TILE, [KF, SEQ], F32R)
        q_all = at("q_all", 0, [KC, SEQ])
        k_all = at("k_all", 4 * TILE, [KC, SEQ])
        v_all = at("v_all", 8 * TILE, [TT, SEQ])
        conv_sq = at("conv_sq", 12 * TILE, [KC, SEQ])
        conv_hi = at("conv_hi", 12 * TILE, [KC, SEQ], F32R)
        conv_raw = at("conv_raw", 16 * TILE, [KC, SEQ])
        conv_lo = at("conv_lo", 16 * TILE, [KC, SEQ], F32R)
        diff_raw = at("diff_raw", 20 * TILE, [KC, SEQ])
        diff_lo = at("diff_lo", 20 * TILE, [KC, SEQ], F32R)
        diff_sq = at("diff_sq", 24 * TILE, [KC, SEQ])
        diff_hi = at("diff_hi", 24 * TILE, [KC, SEQ], F32R)
        chunk_hi = at("chunk_hi", 0, [KC, SEQ], F32R)
        chunk_lo = at("chunk_lo", 4 * TILE, [KC, SEQ], F32R)
        ZPAD = CONV_K - 1
        z = at("z", 20 * TILE, [KC, ZPAD + SEQ])
        conv_odd = at("conv_odd", 25 * TILE, [SEQ])
        q_hi = at("q_hi", 28 * TILE, [SEQ], F32R)
        q_lo = at("q_lo", 29 * TILE, [SEQ], F32R)
        k_hi = at("k_hi", 30 * TILE, [SEQ], F32R)
        k_lo = at("k_lo", 31 * TILE, [SEQ], F32R)
        val_hi = at("val_hi", 32 * TILE, [2, TT, P], F32R)
        val_lo = at("val_lo", 34 * TILE, [2, TT, P], F32R)
        prob = at("prob", 36 * TILE, [2, 2, SEQ])
        pt_hi = at("pt_hi", 40 * TILE, [2, TT, P], F32R)
        pt_lo = at("pt_lo", 42 * TILE, [2, TT, P], F32R)
        mix_hi = at("mix_hi", 28 * TILE, [KD, SEQ], F32R)
        mix_lo = at("mix_lo", 36 * TILE, [KD, SEQ], F32R)

        x = sb("x", [P, KD, SEQ])
        h_hi = sb("h_hi", [P, KD, SEQ], F32R)
        h_lo = sb("h_lo", [P, KD, SEQ], F32R)
        raw = sb("raw", [P, RING, CHUNK])
        w_hi = sb("w_hi", [P, RING, CHUNK], F32R)
        w_lo = sb("w_lo", [P, RING, CHUNK], F32R)
        ymix = sb("ymix", [P, KD, SEQ])
        strip = sb("strip", [P, 2, SEQ])
        ident = sb("ident", [P, P])
        ones = sb("ones", [P, P])
        rbc = sb("rbc", [P, SEQ])
        sqacc = sb("sqacc", [P, SEQ])
        ident_r = sb("ident_r", [P, P], F32R)
        tmp = [sb(f"tmp{i}", [P, SEQ]) for i in range(4)]
        par_all = sb("par_all", [P, DEPTH, N_PAR])
        pr = sb("pr", [P, N_PAR])
        mask_q = sb("mask_q", [P, P], F32R)
        mask_k = sb("mask_k", [P, P // 2], F32R)
        small = sb("small", [P, 64])
        small_r = sb("small_r", [P, 40], F32R)
        r_hi, r_lo = small_r[:, 0:4], small_r[:, 4:8]
        r2_hi, r2_lo = small_r[:, 8:24], small_r[:, 24:40]
        std = small[:, 0:4]
        rtok = small[:, 4:8]
        std2 = small[:, 8:24]
        rtok2 = small[:, 24:40]

        def negmax(par_, c):
            return small[:, 40 + 2 * par_ + c:41 + 2 * par_ + c]

        def rowsum(par_, c):
            return small[:, 44 + 2 * par_ + c:45 + 2 * par_ + c]

        rinv = small[:, 48:50]
        lam_r1 = small[:, 50:51]
        lam_exp = small[:, 52:52 + 2 * DEPTH]
        neg_lam = small[:, 56:56 + DEPTH]
        out_scale = small[:, 58:58 + DEPTH]
        eps_col = small[:, 60:61]
        spare = small[:, 61:62]

        acc = [bank(f"acc{i}") for i in range(4)]
        sc = [bank(f"sc{i}") for i in range(2)]
        tr = bank("tr")
        pv = bank("pv")

        rows = nc.dram_tensor("rows", [DEPTH * HEADS_CHUNK, EXT], F32, kind="Internal")
        ext = nc.dram_tensor("ext", [HEADS_CHUNK, P, EXT], F32, kind="Internal")

        x_landed = [sig(f"x_landed{t}", 0) for t in range(KD)]
        par_landed = sig("par_landed", 0)
        lam_landed = sig("lam_landed", 0)
        rel_landed = sig("rel_landed", 0)
        rows_stored = sig("rows_stored", 0)
        ext_stored = sig("ext_stored", 16)
        out_stored = sig("out_stored", 0)
        zeroed = sig("zeroed", 0)
        ident_done = sig("ident_done", 0)
        consts = sig("consts", 0)
        rel_ready = sig("rel_ready", 0)
        setup = sig("setup", 0)
        lam_prod = sig("lam_prod", 0)
        lam_done = sig("lam_done", 0)
        landed = [sig(f"landed{i}", 16 * CHUNKS // RING) for i in range(RING)]
        tables_landed = sig("tables_landed", 32)
        strip_landed = sig("strip_landed", 16 * KC)

        hi_done = sig("hi_done", CHUNKS)
        split_done = sig("split_done", CHUNKS, RING)
        chunk_used = sig("chunk_used", CHUNKS, RING)

        par_copied = sig("par_copied", 4)
        pair_scaled = sig("pair_scaled", 4 * KF + 2 * KC, 4)
        gate_act = sig("gate_act", 2 * KF + KC)
        act_raw = sig("act_raw", 2 * KF)
        act_hi_done = sig("act_hi_done", 2 * KF)
        act_ready = sig("act_ready", 2 * KF)
        y_evicted = sig("y_evicted", 3 * KD, 2)
        y_squared = sig("y_squared", 3 * KD)
        squared = sig("squared", 3 * KD)
        sq_added = sig("sq_added", 6 * KD)
        summed = sig("summed", 6)
        table_loaded = sig("table_loaded", 3)
        std_ready = sig("std_ready", 6)
        rtok_ready = sig("rtok_ready", 6)
        parts_hi = sig("parts_hi", 9)
        parts_ready = sig("parts_ready", 6)
        bcast = sig("bcast", 6)
        rbc_ready = sig("rbc_ready", 6)
        x_scaled = sig("x_scaled", 4 + KD)
        y_scaled = sig("y_scaled", 2 * (KD - 2))
        x_ready = sig("x_ready", 3 * KD)
        h_hi_done = sig("h_hi_done", 3 * KD)
        h_ready = sig("h_ready", 3 * KD)

        z_padded = sig("z_padded", 1)
        z_ready = sig("z_ready", KC)
        tap_done = sig("tap_done", KC * (CONV_K + 1))
        tables_ready = sig("tables_ready", 2)
        swapped = sig("swapped", 2 * KC)
        cos_part = sig("cos_part", 2 * KC)
        sin_part = sig("sin_part", 2 * KC)
        rope_done = sig("rope_done", 2 * KC)
        v_evicted = sig("v_evicted", 2 * TT)
        cqk_evicted = sig("cqk_evicted", 2 * KC)
        ln_sums = sig("ln_sums", 2)
        ln_mean = sig("ln_mean", 1)
        ln_std = sig("ln_std", 1)
        ln_rstd = sig("ln_rstd", 1)
        ln_parts = sig("ln_parts", 2)
        ln_bcast = sig("ln_bcast", 2)
        ln_centred = sig("ln_centred", KC)
        ln_squared = sig("ln_squared", KC)
        ln_normed = sig("ln_normed", KC)
        conv_act = sig("conv_act", KC)
        conv_hi_done = sig("conv_hi_done", KC)
        u_ready = sig("u_ready", 2 * KC)

        val_zeroed = sig("val_zeroed", 1)
        qk_hi_done = sig("qk_hi_done", 2 * KC)
        qk_staged = sig("qk_staged", 2 * KC)
        val_hi_done = sig("val_hi_done", 2 * KC)
        val_staged = sig("val_staged", 2 * KC)
        scores_done = sig("scores_done", 4 * 16)
        neg_ready = sig("neg_ready", 4 * 16)
        exp_done = sig("exp_done", 4 * 16, 2)
        row_steps = sig("row_steps", 3 * 16 + 16)
        prob_ready = sig("prob_ready", 2 * 16)
        turned = sig("turned", 16 + 32)
        pt_hi_done = sig("pt_hi_done", 16 + 32)
        pt_ready = sig("pt_ready", 16 + 32, 1)
        pv_done = sig("pv_done", 2 * 16, 1)
        o_hi_done = sig("o_hi_done", KC)
        o_evicted = sig("o_evicted", 2 * KC, 1)
        dn_sums = sig("dn_sums", 1)
        dn_std = sig("dn_std", 1)
        dn_rtok = sig("dn_rtok", 2)
        dn_parts = sig("dn_parts", 1)
        dn_bcast = sig("dn_bcast", KC)
        dn_normed = sig("dn_normed", KC)
        dn_hi = sig("dn_hi", KC)

        gate_evicted = sig("gate_evicted", 3 * KD, 2)
        gate_tanh = sig("gate_tanh", 3 * KD)
        out_evicted = sig("out_evicted", 3 * KD, 2)
        mix_added = sig("mix_added", 2 * KD)
        mix_hi_done = sig("mix_hi_done", KD)
        mix_ready = sig("mix_ready", KD)

        block = ctx.enter_context(nc.Block())

        @block.sync
        def _(sp):
            def fetch(lay, n, s, src):
                sp.wait_ge(split_done.sem, split_done.at(lay, n + 1 - RING))
                sp.dma_start(raw[:, s, 0:src.shape[-1]], src).then_inc(landed[s].sem, 16)

            def fetch_ffn(lay, which, c_in, c_out):
                with sp.Fori(0, 2 * KF // RING) as i:
                    for s in range(RING):
                        fetch(lay, c_in + i * RING + s, s, ffn_in[(lay * 2 + which) * (2 * KF) + i * RING + s])
                with sp.Fori(0, KD) as t:
                    for s, (a, b) in enumerate(zip(FFN_OUT_AT[:-1], FFN_OUT_AT[1:])):
                        fetch(lay, c_out + t * RING + s, s, ffn_out[(lay * 2 + which) * KD + t, :, a * P:b * P])

            def fetch_mix(lay, c, n, first):
                with sp.Fori(0, n // RING) as i:
                    for s in range(RING):
                        fetch(lay, c + i * RING + s, s, mix_in[lay * 56 + first + i * RING + s])

            sp.dma_start(par_all[:, :, :], par).then_inc(par_landed.sem, 16)
            sp.dma_start(ymix[0:DEPTH * HEADS_CHUNK, 0:2, :].rearrange("p a b -> p (a b)")[:, EXT_LEFT:EXT_LEFT + N_REL],
                         relb).then_inc(rel_landed.sem, 16)
            sp.dma_start(tmp[0][:, :], lamb.partition_broadcast(P)).then_inc(lam_landed.sem, 16)

            with sp.Fori(0, DEPTH) as lay:
                fetch_ffn(lay, 0, C_FFN1_IN, C_FFN1_OUT)
                fetch_mix(lay, C_GLU, 2 * KC, 0)
                sp.wait_ge(x_ready.sem, x_ready.at(lay, KD))
                for i in range(2):
                    sp.dma_start(ymix[:, i, :], rope[i]).then_inc(tables_landed.sem, 16)
                fetch_mix(lay, C_DQK, 12, 8)
                sp.wait_ge(rows_stored.sem, 16)
                sp.dma_start(ext.ap(), bass.AP(rows, lay * (HEADS_CHUNK * EXT), [[EXT, HEADS_CHUNK], [0, P], [1, EXT]]))\
                    .then_inc(ext_stored.sem, 16)
                with sp.Fori(0, KC) as g:
                    for s in range(RING):
                        fetch(lay, C_A + g * RING + s, s,
                              mix_in[lay * 56 + 20 + g * 2 + s // 2, :, (s % 2) * SEQ:(s % 2 + 1) * SEQ])
                fetch_mix(lay, C_CQK, 12, 28)
                with sp.Fori(0, KC) as g:
                    for s in range(RING):
                        fetch(lay, C_B + g * RING + s, s, mix_in[lay * 56 + 40 + g * 2 + s // 2] if s % 2 == 0
                              else out_ab[lay * KD + g * 2 + s // 2])
                    sp.wait_ge(ext_stored.sem, ext_stored.at(lay, 16))
                    sp.wait_ge(neg_ready.sem, neg_ready.at(lay, 32 + g * 8))
                    sp.dma_start(strip[:, :, :], bass.AP(
                        ext, g * (2 * P * EXT) + P,
                        [[EXT - 1, P], [P * EXT, 2], [1, SEQ]])).then_inc(strip_landed.sem, 16)
                with sp.Fori(0, KC) as g:
                    for s in range(RING):
                        fetch(lay, C_C + g * RING + s, s, mix_in[lay * 56 + 48 + g * 2 + s // 2] if s % 2 == 0
                              else out_c[lay * KD + g * 2 + s // 2])
                with sp.Fori(0, KD // RING) as i:
                    for s in range(RING):
                        fetch(lay, C_WO + i * RING + s, s, wo[lay * KD + i * RING + s])
                fetch_ffn(lay, 1, C_FFN2_IN, C_FFN2_OUT)
            for t in range(KD):
                sp.wait_ge(x_ready.sem, x_ready.at(DEPTH - 1, 2 * KD + t + 1))
                sp.dma_start(outT[:, t, :], x[:, t, :]).then_inc(out_stored.sem, 16)
            sp.wait_ge(out_stored.sem, 16 * KD)

        @block.gpsimd
        def _(pool):
            pool.memset(ident[:, :], 0.0).then_inc(zeroed.sem, 1)
            pool.memset(ones[:, :], 1.0).then_inc(consts.sem, 1)
            pool.memset(mask_q[:, :].bitcast(F32), 0.0).then_inc(zeroed.sem, 1)
            pool.memset(mask_k[:, :].bitcast(F32), 0.0).then_inc(zeroed.sem, 1)
            pool.memset(eps_col, EPS).then_inc(consts.sem, 1)
            for l in range(DEPTH):
                pool.memset(out_scale[:, l:l + 1], 1.0 - lam_init(l)).then_inc(consts.sem, 1)
            pool.wait_ge(zeroed.sem, 3)
            pool.affine_select(out=ident[:, :], in_=ident[:, :], compare_op=ALU.not_equal, fill=1.0, base=0,
                               pattern=[[-1, P]], channel_multiplier=1).then_inc(consts.sem, 1)

            def split_lo(lay, n, s, cols):
                pool.wait_ge(hi_done.sem, hi_done.at(lay, n + 1))
                pool.tensor_tensor(w_lo[:, s, 0:cols], raw[:, s, 0:cols], w_hi[:, s, 0:cols].bitcast(F32),
                                   ALU.subtract).then_inc(split_done.sem, 1)

            def scale_y(lay, sub):
                for t in range(2, KD):
                    pool.wait_ge(rbc_ready.sem, rbc_ready.at(lay, 2 * sub + 2))
                    pool.tensor_tensor(ymix[:, t, :], ymix[:, t, :], rbc[:, :], ALU.mult).then_inc(y_scaled.sem, 1)

            pool.sem_inc(split_done.sem, RING)
            with pool.Fori(0, DEPTH) as lay:
                for a, b in zip(PHASES[:-1], PHASES[1:]):
                    if a in AFTER_NORM:
                        for s in range(RING):
                            split_lo(lay, a + s, s, chunk_cols(a + s))
                        scale_y(lay, AFTER_NORM.index(a))
                        a += RING
                    with pool.Fori(0, (b - a) // RING) as i:
                        for s in range(RING):
                            split_lo(lay, a + i * RING + s, s, chunk_cols(a + s))


        @block.scalar
        def _(act):
            def split_hi(lay, n, s, cols):
                act.wait_ge(landed[s].sem, landed[s].at(lay, n_round(n) * 16 + 16))
                act.wait_ge(chunk_used.sem, chunk_used.at(lay, chunk_at(n) + 1 - RING))
                act.activation(w_hi[:, s, 0:cols], raw[:, s, 0:cols], ACT.Copy).then_inc(hi_done.sem, 1)

            def n_round(n):
                return n // RING if isinstance(n, int) else n[1] + (n[0] + n[2]) // RING

            def chunk_at(n):
                return n if isinstance(n, int) else n[1] * RING + (n[0] + n[2])

            def ahead(lay, c, i, s, last):
                m = s + RING - 1
                if last:
                    n = c + i * RING + m
                    if n < CHUNKS:
                        split_hi(lay, n, n % RING, chunk_cols(n))
                else:
                    split_hi(lay, (c, i, m), m % RING, chunk_cols(c + m))

            def norm_root(lay, k):
                act.wait_ge(summed.sem, summed.at(lay, k + 1))
                act.activation(std, pv[:, 0:TT], ACT.Sqrt, bias=eps_col, scale=1.0 / D_MODEL).then_inc(std_ready.sem, 1)

            def norm_copy(lay, k):
                act.wait_ge(bcast.sem, bcast.at(lay, k + 1))
                act.activation(rbc[:, :], tr[:, :], ACT.Copy).then_inc(rbc_ready.sem, 1)

            def squares(lay, sub, t, src):
                if t >= 2:
                    act.wait_ge(sq_added.sem, sq_added.at(lay, 2 * sub * KD + t - 1))
                act.activation(tmp[2 + t % 2][:, :], src, ACT.Square).then_inc(squared.sem, 1)

            def norm_head(lay, sub):
                g = (0, 2, 4)[sub]
                for t in range(KD):
                    if sub:
                        act.wait_ge(x_ready.sem, x_ready.at(lay, (sub - 1) * KD + t + 1))
                    else:
                        act.wait_ge(x_landed[t].sem, 16)
                    act.activation(h_hi[:, t, :], x[:, t, :], ACT.Copy, scale=pr[:, g * KD + t:g * KD + t + 1])\
                        .then_inc(h_hi_done.sem, 1)
                for t in range(KD):
                    squares(lay, sub, t, x[:, t, :])

            def pairs(lay, c, first_pair, n_pairs, k_norm):
                ffn = n_pairs == KF
                which = 0 if c == C_FFN1_IN else 1

                def pair(i, last, s, j):
                    if isinstance(j, int) and j == 0:
                        split_hi(lay, c + 4, 0, chunk_cols(c + 4))
                        norm_root(lay, k_norm)
                        split_hi(lay, c + 5, 1, chunk_cols(c + 5))
                        norm_copy(lay, k_norm)
                    elif isinstance(j, int) and j == 1:
                        split_hi(lay, c + 6, 2, chunk_cols(c + 6))
                    else:
                        ahead(lay, c, i, s, last)
                    p = first_pair + j
                    act.wait_ge(pair_scaled.sem, pair_scaled.at(lay, 2 * p + 1))
                    if ffn:
                        act.activation(tmp[1][:, :], tmp[0][:, :], ACT.Silu).then_inc(gate_act.sem, 1)
                    else:
                        if j >= 1:
                            act.wait_ge(z_ready.sem, z_ready.at(lay, j))
                        act.activation(tmp[1][:, :], tmp[0][:, :], ACT.Sigmoid).then_inc(gate_act.sem, 1)
                    if not (isinstance(j, int) and j <= 1):
                        ahead(lay, c, i, s + 1, last)
                    if ffn:
                        act.wait_ge(act_raw.sem, act_raw.at(lay, which * KF + j + 1))
                        act.activation(act_hi[:, j, :], tmp[3][:, :], ACT.Copy).then_inc(act_hi_done.sem, 1)

                n = n_pairs // 2
                pair(0, False, 0, 0)
                pair(0, False, 2, 1)
                if n > 2:
                    with act.Fori(1, n - 1) as i:
                        pair(i, False, 0, i * 2)
                        pair(i, False, 2, i * 2 + 1)
                pair(n - 1, True, 0, 2 * n - 2)
                pair(n - 1, True, 2, 2 * n - 1)

            def y_tile(lay, sub, t, bank_, n_used, parity):
                act.wait_ge(chunk_used.sem, chunk_used.at(lay, n_used))
                if not isinstance(t, int) or t >= 2:
                    act.wait_ge(sq_added.sem, sq_added.at(lay, (2 * sub + 1) * KD + t - 1))
                act.activation(tmp[2 + parity][:, :], bank_[:, :], ACT.Square).then_inc(y_squared.sem, 1)
                act.activation(ymix[:, t, :], bank_[:, :], ACT.Copy).then_inc(y_evicted.sem, 1)

            def root_table(lay, k):
                act.wait_ge(rbc_ready.sem, rbc_ready.at(lay, k))
                act.activation(spare, eps_col, ACT.Sqrt).then_inc(table_loaded.sem, 1)

            def ffn_out_tiles(lay, sub, c):
                def two(i, last, t):
                    for s in range(2 * RING):
                        ahead(lay, c, i * 2, s, last)
                        if last and s == 2 * RING - 1:
                            root_table(lay, 2 * sub + 1)
                        if s % RING == RING - 1:
                            y_tile(lay, sub, t + s // RING, acc[s // RING], c + RING + t * RING + s // RING * RING,
                                   s // RING)
                two(0, False, 0)
                with act.Fori(1, KD // 2 - 1) as i:
                    two(i, False, i * 2)
                two(KD // 2 - 1, True, KD - 2)

            def rope_swap(lay, j, bank_, scale, n):
                act.wait_ge(chunk_used.sem, chunk_used.at(lay, n + 1))
                if j >= 2:
                    act.wait_ge(rope_done.sem, rope_done.at(lay, j - 1))
                else:
                    act.wait_ge(z_ready.sem, z_ready.at(lay, KC))
                for g in range(4):
                    o = act.activation(tmp[j % 2][32 * (g ^ 1):32 * (g ^ 1) + 32, :],
                                       bank_[32 * g:32 * g + 32, :], ACT.Copy, scale=scale)
                o.then_inc(swapped.sem, 1)

            def values(lay, c):
                for s in range(RING):
                    ahead(lay, c, 0, s, True)
                act.wait_ge(chunk_used.sem, chunk_used.at(lay, c + RING))
                for t in range(TT):
                    act.activation(v_all[:, t, :], acc[t][:, :], ACT.Copy, scale=rtok[:, t:t + 1])\
                        .then_inc(v_evicted.sem, 1)

            def conv_squares(lay):
                for t in range(KC):
                    act.wait_ge(ln_centred.sem, ln_centred.at(lay, t + 1))
                    act.activation(conv_sq[:, t, :], conv_raw[:, t, :], ACT.Square).then_inc(ln_squared.sem, 1)

            def conv_root(lay):
                act.wait_ge(ln_sums.sem, ln_sums.at(lay, 2))
                act.activation(std2[:, 0:TT], acc[2][:, 0:TT], ACT.Sqrt, bias=eps_col, scale=1.0 / C_CONV)\
                    .then_inc(ln_std.sem, 1)

            def conv_silu(lay):
                for t in range(KC):
                    act.wait_ge(ln_normed.sem, ln_normed.at(lay, t + 1))
                    act.activation(conv_raw[:, t, :], conv_raw[:, t, :], ACT.Silu,
                                   bias=pr[:, PAR_LN + KC + t:PAR_LN + KC + t + 1],
                                   scale=pr[:, PAR_LN + t:PAR_LN + t + 1]).then_inc(conv_act.sem, 1)
                for t in range(KC):
                    act.wait_ge(conv_act.sem, conv_act.at(lay, t + 1))
                    act.activation(conv_hi[:, t, :], conv_raw[:, t, :], ACT.Copy).then_inc(conv_hi_done.sem, 1)

            def after_y(lay, k, c):
                split_hi(lay, c + 3, 3, CHUNK)
                norm_root(lay, k)
                norm_copy(lay, k)

            def diff_norm(lay):
                act.wait_ge(dn_sums.sem, dn_sums.at(lay, 1))
                act.activation(std2, pv[:, 0:16], ACT.Sqrt, bias=eps_col, scale=1.0 / P).then_inc(dn_std.sem, 1)

            def stage_qk(h):
                act.activation(q_hi[:, :], q_all[:, h, :], ACT.Copy)
                act.activation(k_hi[:, :], k_all[:, h, :], ACT.Copy).then_inc(qk_hi_done.sem, 1)

            def attention(lay, kind, c):
                U0, H0, S0, T0 = 16 * kind, KC * kind, 32 * kind, 16 * kind
                n_comp = 1 + kind

                def turn_unit(h, u):
                    hp, up = (h, u - 1) if u else (h - 1, 3)
                    for comp in range(n_comp):
                        m = T0 + n_comp * (hp * 4 + up) + comp
                        act.wait_ge(turned.sem, turned.at(lay, m + 1))
                        act.wait_ge(pv_done.sem, pv_done.at(lay, U0 + hp * 4 + up))
                        w = (up + 1) * P
                        act.activation(pt_hi[:, comp, 0:up + 1, :].rearrange("p a b -> p (a b)"), tr[:, 0:w], ACT.Copy)\
                            .then_inc(pt_hi_done.sem, 1)

                def outputs(hp):
                    act.wait_ge(pv_done.sem, pv_done.at(lay, U0 + hp * 4 + 4))
                    if kind == 0:
                        act.activation(diff_raw[:, hp, :], pv[:, :], ACT.Copy)
                        act.activation(diff_sq[:, (KC - 1) - hp, :], pv[:, :], ACT.Square).then_inc(o_evicted.sem, 1)
                    else:
                        act.activation(chunk_hi[:, hp, :], pv[:, :], ACT.Copy).then_inc(o_hi_done.sem, 1)

                def tanh_a(t, e):
                    act.wait_ge(gate_evicted.sem, gate_evicted.at(lay, t + 1))
                    act.activation(ymix[:, t, :], tmp[e][:, :], ACT.Tanh,
                                   bias=pr[:, bass.ds(PAR_GATE_B + t, 1)], scale=0.5).then_inc(gate_tanh.sem, 1)

                def head(h, first, last):
                    for u in range(4):
                        w = (u + 1) * P
                        for comp in range(2):
                            act.wait_ge(neg_ready.sem, neg_ready.at(lay, S0 + h * 8 + (2 * u + comp + 1)))
                            if kind == 0:
                                if u >= 2 or not first:
                                    act.wait_ge(turned.sem, turned.at(lay, h * 4 + (u - 1)))
                                act.activation(prob[:, u % 2, comp, 0:w], sc[comp][:, 0:w], ACT.Exp,
                                               bias=negmax(u % 2, comp), accum_out=rowsum(u % 2, comp))\
                                    .then_inc(exp_done.sem, 1)
                            else:
                                act.activation(prob[:, u % 2, comp, 0:w], prob[:, u % 2, comp, 0:w], ACT.Exp,
                                               bias=negmax(u % 2, comp), scale=-1.0, accum_out=rowsum(u % 2, comp))\
                                    .then_inc(exp_done.sem, 1)
                        if u == 1:
                            if not first:
                                outputs(h - 1)
                            stage_values(h, first)
                        if u or not first:
                            turn_unit(h, u)
                        if u == 3 and not last:
                            act.wait_ge(scores_done.sem, scores_done.at(lay, S0 + h * 8 + 8))
                            stage_qk(h + 1)
                        ahead(lay, c, h, u, last)
                        if kind == 0 and u % 2 == 0 and not (first and u == 0):
                            tanh_a(h * 2 + (u // 2 - 1), (u // 2 + 1) % 2)
                        if kind == 1 and u % 2:
                            tanh_gate(lay, 1, h * 2 + u // 2, u // 2)
                        if kind == 0 and last and u:
                            (conv_squares, conv_root, conv_silu)[u - 1](lay)

                def stage_values(h, first):
                    if kind == 0:
                        if first:
                            act.wait_ge(v_evicted.sem, v_evicted.at(lay, TT))
                        act.activation(val_hi[:, 0, :, :], v_all[:, :, head_cols(h)], ACT.Copy)\
                            .then_inc(val_hi_done.sem, 1)
                    else:
                        for comp in range(2):
                            if first and comp == 0:
                                act.wait_ge(v_evicted.sem, v_evicted.at(lay, 2 * TT))
                            o = act.activation(val_hi[:, comp, :, 64 * comp:64 * comp + 64],
                                               v_all[:, :, head_cols(h, comp)], ACT.Copy)
                        o.then_inc(val_hi_done.sem, 1)

                head(0, True, False)
                with act.Fori(1, KC - 1) as h:
                    head(h, False, False)
                head(KC - 1, False, True)
                turn_unit(KC, 0)
                if kind == 0:
                    tanh_a(KD - 1, 1)
                outputs(KC - 1)

            def head_cols(h, comp=None):
                return bass.ds(h * P, P) if comp is None else bass.ds(h * P + 64 * comp, 64)

            def tanh_gate(lay, branch, t, par_):
                act.wait_ge(gate_evicted.sem, gate_evicted.at(lay, branch * KD + t + 1))
                act.activation(tmp[2 + par_][:, :], tmp[par_][:, :], ACT.Tanh,
                               bias=pr[:, bass.ds(PAR_GATE_B + branch * KD + t, 1)], scale=0.5).then_inc(gate_tanh.sem, 1)

            for t in range(KD):
                act.dma_start(x[:, t, :], xT[:, t, :]).then_inc(x_landed[t].sem, 16)
            act.wait_ge(par_landed.sem, 16)
            act.wait_ge(consts.sem, N_CONSTS)
            act.wait_ge(lam_prod.sem, 2)
            act.activation(lam_exp, tmp[1][:, 256:256 + 2 * DEPTH], ACT.Exp).then_inc(lam_done.sem, 1)
            act.sem_inc(exp_done.sem, 2)
            act.wait_ge(rel_ready.sem, 2)
            row = ymix[0:DEPTH * HEADS_CHUNK, 0:2, :].rearrange("p a b -> p (a b)")[:, 0:EXT]
            act.dma_start(rows.ap(), row).then_inc(rows_stored.sem, 16)

            with act.Fori(0, DEPTH) as lay:
                for n in range(RING - 1):
                    split_hi(lay, n, n, chunk_cols(n))
                split_hi(lay, RING - 1, RING - 1, CHUNK)
                act.wait_ge(par_copied.sem, par_copied.at(lay, 4))
                norm_head(lay, 0)
                pairs(lay, C_FFN1_IN, 0, KF, 0)
                act.wait_ge(rows_stored.sem, 16)
                ffn_out_tiles(lay, 0, C_FFN1_OUT)
                after_y(lay, 1, C_GLU)
                norm_head(lay, 1)
                pairs(lay, C_GLU, KF, KC, 2)
                for i in range(2):
                    for s in range(RING):
                        j = i * RING + s
                        ahead(lay, C_DQK, i, s, i == 1)
                        rope_swap(lay, j, acc[s], ATT_SCALE if i == 0 else 1.0, C_DQK + j)
                act.wait_ge(rope_done.sem, rope_done.at(lay, 2 * KC))
                stage_qk(0)
                values(lay, C_DV)
                attention(lay, 0, C_A)
                for i in range(2):
                    for s in range(RING):
                        ahead(lay, C_CQK, i, s, i == 1)
                        j = i * RING + s
                        if j == 0:
                            diff_norm(lay)
                        elif j <= KC:
                            act.wait_ge(dn_normed.sem, dn_normed.at(lay, j))
                            act.activation(diff_hi[:, j - 1, :], diff_raw[:, j - 1, :], ACT.Copy).then_inc(dn_hi.sem, 1)
                act.wait_ge(scores_done.sem, scores_done.at(lay, 32))
                act.wait_ge(cqk_evicted.sem, cqk_evicted.at(lay, 2 * KC))
                stage_qk(0)
                values(lay, C_CV)
                attention(lay, 1, C_B)

                def last_branch(i, last):
                    for s in range(RING):
                        ahead(lay, C_C, i, s, last)
                        if s % 2:
                            t = i * 2 + s // 2
                            tanh_gate(lay, 2, t, s // 2)
                            act.wait_ge(mix_added.sem, mix_added.at(lay, KD + t + 1))
                            act.activation(mix_hi[:, t, :], ymix[:, t, :], ACT.Copy, scale=0.5)\
                                .then_inc(mix_hi_done.sem, 1)
                with act.Fori(0, KC - 1) as i:
                    last_branch(i, False)
                last_branch(KC - 1, True)
                for i in range(KD // RING):
                    for s in range(RING):
                        t = i * RING + s
                        ahead(lay, C_WO, i, s, i == KD // RING - 1)
                        if t == KD - 1:
                            root_table(lay, 3)
                        y_tile(lay, 1, t, acc[t % 2], C_WO + t + 1, t % 2)
                after_y(lay, 3, C_FFN2_IN)
                norm_head(lay, 2)
                pairs(lay, C_FFN2_IN, KF + KC, KF, 4)
                ffn_out_tiles(lay, 2, C_FFN2_OUT)
                norm_root(lay, 5)
                norm_copy(lay, 5)

        @block.vector
        def _(dve):
            def f32(ap):
                return ap.bitcast(F32)

            def par_col(k):
                return pr[:, k:k + 1]

            def sum_squares(lay, g, signal, k):
                for t in range(KD):
                    dve.wait_ge(signal.sem, signal.at(lay, k + t + 1))
                    if t == 0:
                        dve.tensor_copy(sqacc[:, :], tmp[2][:, :]).then_inc(sq_added.sem, 1)
                    else:
                        dve.wait_ge(sq_added.sem, sq_added.at(lay, g * KD + t))
                        dve.tensor_tensor(sqacc[:, :], sqacc[:, :], tmp[2 + t % 2][:, :], ALU.add)\
                            .then_inc(sq_added.sem, 1)

            def parts(lay, n, col, hi, lo, signal):
                dve.tensor_copy(hi, col).then_inc(parts_hi.sem, 1)
                dve.wait_ge(parts_hi.sem, parts_hi.at(lay, n + 1))
                dve.tensor_tensor(lo, col, f32(hi), ALU.subtract).then_inc(signal.sem, 1)

            def norm_scalar(lay, k):
                dve.wait_ge(std_ready.sem, std_ready.at(lay, k + 1))
                dve.reciprocal(rtok, std).then_inc(rtok_ready.sem, 1)
                dve.wait_ge(rtok_ready.sem, rtok_ready.at(lay, k + 1))
                parts(lay, k if k < 3 else k + 3, rtok, r_hi, r_lo, parts_ready)

            def h_low(lay, sub, t):
                g = (0, 2, 4)[sub]
                dve.wait_ge(h_hi_done.sem, h_hi_done.at(lay, sub * KD + t + 1))
                dve.scalar_tensor_tensor(h_lo[:, t, :], x[:, t, :], par_col(g * KD + t), f32(h_hi[:, t, :]),
                                         ALU.mult, ALU.subtract).then_inc(h_ready.sem, 1)

            def add_to_x(lay, sub, t, y):
                g = (1, 3, 5)[sub]
                dve.scalar_tensor_tensor(x[:, t, :], y, par_col(g * KD + t), x[:, t, :], ALU.mult, ALU.add)\
                    .then_inc(x_ready.sem, 1)

            def residual(lay, sub):
                dve.wait_ge(rbc_ready.sem, rbc_ready.at(lay, 2 * sub + 2))
                for t in range(KD):
                    if t < 2:
                        dve.wait_ge(y_evicted.sem, y_evicted.at(lay, sub * KD + t + 1))
                        dve.tensor_tensor(tmp[t][:, :], ymix[:, t, :], rbc[:, :], ALU.mult).then_inc(x_scaled.sem, 1)
                        dve.wait_ge(x_scaled.sem, x_scaled.at(lay, 2 * sub + t + 1))
                        add_to_x(lay, sub, t, tmp[t][:, :])
                    else:
                        dve.wait_ge(y_scaled.sem, y_scaled.at(lay, (KD - 2) * sub + t - 1))
                        add_to_x(lay, sub, t, ymix[:, t, :])
                    if t:
                        h_low(lay, sub + 1, t - 1)
                h_low(lay, sub + 1, KD - 1)

            def last_residual(lay):
                dve.wait_ge(rbc_ready.sem, rbc_ready.at(lay, 6))
                for t in range(KD + 1):
                    if t < KD:
                        if t >= 2:
                            dve.wait_ge(x_ready.sem, x_ready.at(lay, 2 * KD + t - 1))
                        dve.tensor_tensor(tmp[t % 2][:, :], ymix[:, t, :], rbc[:, :], ALU.mult).then_inc(x_scaled.sem, 1)
                    if t >= 1:
                        dve.wait_ge(x_scaled.sem, x_scaled.at(lay, 4 + t))
                        add_to_x(lay, 2, t - 1, tmp[(t - 1) % 2][:, :])
                dve.wait_ge(x_ready.sem, x_ready.at(lay, 3 * KD))

            def ffn_pair(lay, which, c, first_pair, j, b):
                p = first_pair + j
                k = which * KF + j
                dve.wait_ge(rbc_ready.sem, rbc_ready.at(lay, 4 * which + 1))
                dve.wait_ge(chunk_used.sem, chunk_used.at(lay, c + j * 2 + 2))
                dve.tensor_tensor(tmp[0][:, :], acc[b][:, :], rbc[:, :], ALU.mult).then_inc(pair_scaled.sem, 1)
                dve.tensor_tensor(tmp[2][:, :], acc[b + 1][:, :], rbc[:, :], ALU.mult).then_inc(pair_scaled.sem, 1)
                dve.wait_ge(gate_act.sem, gate_act.at(lay, k + (KC if which else 0) + 1))
                dve.wait_ge(pair_scaled.sem, pair_scaled.at(lay, p * 2 + 2))
                dve.tensor_tensor(tmp[3][:, :], tmp[1][:, :], tmp[2][:, :], ALU.mult).then_inc(act_raw.sem, 1)
                dve.wait_ge(act_hi_done.sem, act_hi_done.at(lay, k + 1))
                dve.tensor_tensor(act_lo[:, j, :], tmp[3][:, :], f32(act_hi[:, j, :]), ALU.subtract)\
                    .then_inc(act_ready.sem, 1)

            def ffn(lay, which, c, first_pair):
                with dve.Fori(0, KF // 2) as i:
                    for e in range(2):
                        ffn_pair(lay, which, c, first_pair, i * 2 + e, 2 * e)
                sum_squares(lay, 4 * which + 1, y_squared, 2 * which * KD)
                norm_scalar(lay, 4 * which + 1)

            def conv_taps(lay, i, taps):
                if taps[0] == 0:
                    dve.wait_ge(z_ready.sem, z_ready.at(lay, i + 1))
                    dve.wait_ge(z_padded.sem, z_padded.at(lay, 1))
                for k in taps:
                    w = par_col(PAR_DW + i * CONV_K + k)
                    to = conv_raw[:, i, :] if k % 2 == 0 else conv_odd[:, :]
                    src = z[:, i, k:k + SEQ]
                    if k == 0:
                        o = dve.tensor_scalar(to, src, w, par_col(PAR_CONV_B + i), ALU.mult, ALU.add)
                    elif k == 1:
                        if i:
                            dve.wait_ge(tap_done.sem, tap_done.at(lay, i * (CONV_K + 1)))
                        o = dve.tensor_scalar(to, src, w, None, ALU.mult)
                    else:
                        dve.wait_ge(tap_done.sem, tap_done.at(lay, i * (CONV_K + 1) + k - 1))
                        o = dve.scalar_tensor_tensor(to, src, w, to, ALU.mult, ALU.add)
                    o.then_inc(tap_done.sem, 1)
                if taps[-1] == CONV_K - 1:
                    add_odd(lay, i)

            def add_odd(lay, i):
                dve.wait_ge(tap_done.sem, tap_done.at(lay, i * (CONV_K + 1) + CONV_K))
                dve.tensor_tensor(conv_raw[:, i, :], conv_raw[:, i, :], conv_odd[:, :], ALU.add).then_inc(tap_done.sem, 1)

            def later_taps(lay, h, taps):
                n_first = FIRST_TAPS[-1][-1] + 1
                for m in taps:
                    k = h * HEAD_TAPS + (n_first - HEAD_TAPS + m)
                    to = conv_raw[:, KC - 1, :] if (n_first + m) % 2 == 0 else conv_odd[:, :]
                    dve.wait_ge(tap_done.sem, tap_done.at(lay, k + ((KC - 1) * (CONV_K + 1) - 1)))
                    dve.scalar_tensor_tensor(to, z[:, KC - 1, bass.ds(k, SEQ)],
                                             pr[:, bass.ds(k + (PAR_DW + (KC - 1) * CONV_K), 1)], to,
                                             ALU.mult, ALU.add).then_inc(tap_done.sem, 1)

            def stage_qk(lay, kind, h):
                dve.wait_ge(qk_hi_done.sem, qk_hi_done.at(lay, h + (KC * kind + 1)))
                dve.tensor_tensor(q_lo[:, :], q_all[:, h, :], f32(q_hi[:, :]), ALU.subtract)
                dve.tensor_tensor(k_lo[:, :], k_all[:, h, :], f32(k_hi[:, :]), ALU.subtract)\
                    .then_inc(qk_staged.sem, 1)

            def glu(lay):
                dve.memset(z[:, :, 0:ZPAD], 0.0).then_inc(z_padded.sem, 1)
                dve.wait_ge(rbc_ready.sem, rbc_ready.at(lay, 3))
                for j in range(KC):
                    b = 2 * (j % 2)
                    dve.wait_ge(chunk_used.sem, chunk_used.at(lay, C_GLU + 2 * j + 2))
                    if j:
                        dve.wait_ge(z_ready.sem, z_ready.at(lay, j))
                    dve.tensor_tensor(tmp[0][:, :], acc[b + 1][:, :], rbc[:, :], ALU.mult).then_inc(pair_scaled.sem, 1)
                    dve.tensor_tensor(tmp[2][:, :], acc[b][:, :], rbc[:, :], ALU.mult).then_inc(pair_scaled.sem, 1)
                    dve.wait_ge(gate_act.sem, gate_act.at(lay, KF + j + 1))
                    dve.wait_ge(pair_scaled.sem, pair_scaled.at(lay, 2 * (KF + j) + 2))
                    dve.tensor_tensor(z[:, j, ZPAD:ZPAD + SEQ], tmp[1][:, :], tmp[2][:, :], ALU.mult)\
                        .then_inc(z_ready.sem, 1)
                    if j >= 1:
                        conv_taps(lay, (j - 1) // 2, HALVES[(j - 1) % 2])

            def rope_and_conv(lay):
                dve.wait_ge(tables_landed.sem, tables_landed.at(lay, 32))
                for i in range(2):
                    dve.tensor_tensor(ymix[:, i, :], ymix[:, i, :], rbc[:, :], ALU.mult).then_inc(tables_ready.sem, 1)
                dve.wait_ge(tables_ready.sem, tables_ready.at(lay, 2))
                for j in range(2 * KC):
                    to = (q_all if j < KC else k_all)[:, j % KC, :]
                    dve.wait_ge(swapped.sem, swapped.at(lay, j + 1))
                    dve.scalar_tensor_tensor(to, acc[j % 4][:, :], ATT_SCALE if j < KC else 1.0, ymix[:, 0, :],
                                             ALU.mult, ALU.mult).then_inc(cos_part.sem, 1)
                    dve.tensor_tensor(tmp[j % 2][:, :], tmp[j % 2][:, :], ymix[:, 1, :], ALU.mult).then_inc(sin_part.sem, 1)
                    dve.wait_ge(cos_part.sem, cos_part.at(lay, j + 1))
                    dve.wait_ge(sin_part.sem, sin_part.at(lay, j + 1))
                    dve.tensor_tensor(to, to, tmp[j % 2][:, :], ALU.add).then_inc(rope_done.sem, 1)
                    if 1 <= j <= len(ROPE_TAPS):
                        conv_taps(lay, 1, ROPE_TAPS[j - 1])
                stage_qk(lay, 0, 0)
                conv_taps(lay, 2, range(CONV_K))

            def conv_mean(lay):
                dve.wait_ge(ln_sums.sem, ln_sums.at(lay, 1))
                dve.tensor_scalar(rtok2[:, 0:TT], acc[2][:, 0:TT], 1.0 / C_CONV, None, ALU.mult).then_inc(ln_mean.sem, 1)
                dve.wait_ge(ln_mean.sem, ln_mean.at(lay, 1))
                parts(lay, 3, rtok2[:, 0:TT], r2_hi[:, 0:TT], r2_lo[:, 0:TT], ln_parts)

            def conv_centre(lay):
                dve.wait_ge(ln_bcast.sem, ln_bcast.at(lay, 1))
                for t in range(KC):
                    dve.tensor_tensor(conv_raw[:, t, :], conv_raw[:, t, :], acc[3][:, :], ALU.subtract)\
                        .then_inc(ln_centred.sem, 1)

            def conv_rstd(lay):
                dve.wait_ge(ln_std.sem, ln_std.at(lay, 1))
                dve.reciprocal(rtok2[:, 0:TT], std2[:, 0:TT]).then_inc(ln_rstd.sem, 1)
                dve.wait_ge(ln_rstd.sem, ln_rstd.at(lay, 1))
                parts(lay, 4, rtok2[:, 0:TT], r2_hi[:, 0:TT], r2_lo[:, 0:TT], ln_parts)

            def conv_scale(lay):
                dve.wait_ge(ln_bcast.sem, ln_bcast.at(lay, 2))
                dve.wait_ge(ln_centred.sem, ln_centred.at(lay, KC))
                for t in range(KC):
                    dve.tensor_tensor(conv_raw[:, t, :], conv_raw[:, t, :], acc[3][:, :], ALU.mult)\
                        .then_inc(ln_normed.sem, 1)

            def conv_low(lay):
                for t in range(KC):
                    dve.wait_ge(conv_hi_done.sem, conv_hi_done.at(lay, t + 1))
                    dve.tensor_tensor(conv_lo[:, t, :], conv_raw[:, t, :], f32(conv_hi[:, t, :]), ALU.subtract)\
                        .then_inc(u_ready.sem, 1)

            def diff_norm_scalars(lay):
                dve.wait_ge(dn_std.sem, dn_std.at(lay, 1))
                dve.reciprocal(rtok2, std2).then_inc(dn_rtok.sem, 1)
                dve.wait_ge(dn_rtok.sem, dn_rtok.at(lay, 1))
                dve.tensor_scalar(rtok2, rtok2, out_scale[:, bass.ds(lay, 1)], None, ALU.mult).then_inc(dn_rtok.sem, 1)
                dve.wait_ge(dn_rtok.sem, dn_rtok.at(lay, 2))
                parts(lay, 5, rtok2, r2_hi, r2_lo, dn_parts)

            def diff_norm(lay, h):
                dve.wait_ge(dn_bcast.sem, dn_bcast.at(lay, h + 1))
                dve.tensor_tensor(diff_raw[:, h, :], diff_raw[:, h, :], tr[:, :], ALU.mult).then_inc(dn_normed.sem, 1)
                dve.wait_ge(dn_hi.sem, dn_hi.at(lay, h + 1))
                dve.tensor_tensor(diff_lo[:, h, :], diff_raw[:, h, :], f32(diff_hi[:, h, :]), ALU.subtract)\
                    .then_inc(u_ready.sem, 1)

            def chunk_qk(lay):
                for j in range(2 * KC):
                    to = (q_all if j < KC else k_all)[:, j % KC, :]
                    dve.wait_ge(chunk_used.sem, chunk_used.at(lay, C_CQK + j + 1))
                    dve.scalar_tensor_tensor(to, acc[j % 4][:, :], ATT_SCALE if j < KC else 1.0, rbc[:, :],
                                             ALU.mult, ALU.mult).then_inc(cqk_evicted.sem, 1)
                    if j == 0:
                        diff_norm_scalars(lay)
                    if 1 <= j <= KC:
                        diff_norm(lay, j - 1)
                stage_qk(lay, 1, 0)

            def gate_evict(lay, branch, t, b, n_used):
                dve.wait_ge(chunk_used.sem, chunk_used.at(lay, n_used))
                k = branch * KD + t
                if branch == 2:
                    dve.wait_ge(mix_added.sem, mix_added.at(lay, t + (KD - 1)))
                elif branch == 1 and not (isinstance(t, int) and t < 2):
                    dve.wait_ge(mix_added.sem, mix_added.at(lay, t - 1))
                elif branch == 1 or not (isinstance(t, int) and t < 2):
                    dve.wait_ge(gate_tanh.sem, gate_tanh.at(lay, k - 1))
                dve.tensor_tensor(tmp[b][:, :], acc[b][:, :], rbc[:, :], ALU.mult).then_inc(gate_evicted.sem, 1)

            def mix_first(lay, t):
                dve.wait_ge(gate_tanh.sem, gate_tanh.at(lay, t + 1))
                dve.scalar_tensor_tensor(ymix[:, t, :], ymix[:, t, :], 1.0, acc[2][:, :], ALU.add, ALU.mult)\
                    .then_inc(out_evicted.sem, 1)

            def mix_next(lay, branch, t, b, bank_, k_out):
                dve.wait_ge(gate_tanh.sem, gate_tanh.at(lay, branch * KD + t + 1))
                dve.scalar_tensor_tensor(tmp[b][:, :], tmp[2 + b][:, :], 1.0, bank_[:, :], ALU.add, ALU.mult)\
                    .then_inc(out_evicted.sem, 1)
                dve.wait_ge(out_evicted.sem, out_evicted.at(lay, k_out + 1))
                dve.tensor_tensor(ymix[:, t, :], ymix[:, t, :], tmp[b][:, :], ALU.add).then_inc(mix_added.sem, 1)

            def outs_ab(lay, t, b):
                dve.wait_ge(chunk_used.sem, chunk_used.at(lay, C_B + 2 + t * 2))
                mix_first(lay, t)
                mix_next(lay, 1, t, b, acc[3], t * 2 + 1)

            def attention(lay, kind, c, part):
                U0, H0, S0, T0 = 16 * kind, KC * kind, 32 * kind, 16 * kind
                n_comp = 1 + kind

                def turn_unit(h, u):
                    hp, up = (h, u - 1) if u else (h - 1, 3)
                    w = (up + 1) * P
                    for comp in range(n_comp):
                        m = (hp * 4 + up) * n_comp + (T0 + comp)
                        dve.wait_ge(pt_hi_done.sem, pt_hi_done.at(lay, m + 1))
                        dve.tensor_tensor(pt_lo[:, comp, 0:up + 1, :].rearrange("p a b -> p (a b)"), tr[:, 0:w],
                                          f32(pt_hi[:, comp, 0:up + 1, :]).rearrange("p a b -> p (a b)"), ALU.subtract)\
                            .then_inc(pt_ready.sem, 1)

                def outputs(hp):
                    dve.wait_ge(o_hi_done.sem, o_hi_done.at(lay, hp + 1))
                    dve.tensor_tensor(chunk_lo[:, hp, :], pv[:, :], f32(chunk_hi[:, hp, :]), ALU.subtract)\
                        .then_inc(o_evicted.sem, 1)

                def stage_values(h):
                    dve.wait_ge(val_hi_done.sem, val_hi_done.at(lay, h + (H0 + 1)))
                    if kind == 0:
                        dve.tensor_tensor(val_lo[:, 0, :, :], v_all[:, :, bass.ds(h * P, P)], f32(val_hi[:, 0, :, :]),
                                          ALU.subtract).then_inc(val_staged.sem, 1)
                        return
                    for comp in range(2):
                        to = slice(64 * comp, 64 * comp + 64)
                        o = dve.tensor_tensor(val_lo[:, comp, :, to], v_all[:, :, bass.ds(h * P + 64 * comp, 64)],
                                              f32(val_hi[:, comp, :, to]), ALU.subtract)
                    o.then_inc(val_staged.sem, 1)

                def beside(h, u, first):
                    if kind == 0 and u % 2 == 0 and not (first and u == 0):
                        t = h * 2 + (u // 2 - 1)
                        gate_evict(lay, 0, t, (u // 2 + 1) % 2, C_A + 2 + t * 2)
                    if kind == 1 and u % 2:
                        t = h * 2 + u // 2
                        gate_evict(lay, 1, t, u // 2, C_B + 1 + t * 2)
                    if kind == 1 and u % 2 == 0 and not (first and u == 0):
                        outs_ab(lay, h * 2 + (u // 2 - 1), (u // 2 + 1) % 2)

                def head(h, first, last):
                    for u in range(4):
                        w = (u + 1) * P
                        even = u % 2
                        if u == 0 and kind == 0 and last:
                            add_odd(lay, KC - 1)
                        if u == 0 and kind == 1:
                            dve.wait_ge(strip_landed.sem, strip_landed.at(lay, h * 16 + 16))
                        for comp in range(2):
                            dve.wait_ge(scores_done.sem, scores_done.at(lay, h * 8 + (S0 + 2 * u + comp + 1)))
                            if kind == 0:
                                dve.tensor_reduce(negmax(even, comp), sc[comp][:, 0:w], AX.X, ALU.max, negate=True)\
                                    .then_inc(neg_ready.sem, 1)
                            else:
                                if comp == 0:
                                    dve.wait_ge(turned.sem, turned.at(lay, 16 if first and u < 2 else (h * 8 + (16 + 2 * u - 2))))
                                dve.memset(rowsum(even, comp), 0.0)
                                dve.tensor_tensor_reduce(prob[:, even, comp, 0:w], sc[comp][:, 0:w],
                                                         strip[:, comp, SEQ - w:SEQ], -1.0, 3.0e38, ALU.add, ALU.min,
                                                         negmax(even, comp)).then_inc(neg_ready.sem, 1)
                        if u == 1:
                            if not first and kind == 1:
                                outputs(h - 1)
                            stage_values(h)
                        beside(h, u, first)
                        if kind == 0 and first:
                            conv_taps(lay, KC - 1, FIRST_TAPS[u])
                        elif kind == 0 and not last and u < 3:
                            later_taps(lay, h, LATER_TAPS[u])
                        if u or not first:
                            turn_unit(h, u)
                        if u == 3 and not last:
                            stage_qk(lay, kind, h + 1)
                        dve.wait_ge(exp_done.sem, exp_done.at(lay, h * 8 + (S0 + 2 * u + 2)))
                        steps = (h * 12 + 3 * u) if kind == 0 else (h * 4 + (48 + u))
                        if kind or u or not first:
                            dve.wait_ge(prob_ready.sem, prob_ready.at(lay, h * 4 + (U0 + u)))
                        dve.reciprocal(rinv, small[:, 44 + 2 * even:46 + 2 * even]).then_inc(row_steps.sem, 1)
                        dve.wait_ge(row_steps.sem, row_steps.at(lay, steps + 1))
                        if kind == 0:
                            dve.tensor_scalar(lam_r1, rinv[:, 1:2], neg_lam[:, bass.ds(lay, 1)], None, ALU.mult)\
                                .then_inc(row_steps.sem, 1)
                            dve.tensor_scalar(prob[:, even, 0, 0:w], prob[:, even, 0, 0:w], rinv[:, 0:1], None, ALU.mult)\
                                .then_inc(row_steps.sem, 1)
                            dve.wait_ge(row_steps.sem, row_steps.at(lay, steps + 3))
                            dve.scalar_tensor_tensor(prob[:, even, 0, 0:w], prob[:, even, 1, 0:w], lam_r1,
                                                     prob[:, even, 0, 0:w], ALU.mult, ALU.add).then_inc(prob_ready.sem, 1)
                        else:
                            for comp in range(2):
                                o = dve.tensor_scalar(prob[:, even, comp, 0:w], prob[:, even, comp, 0:w],
                                                      rinv[:, comp:comp + 1], None, ALU.mult)
                            o.then_inc(prob_ready.sem, 1)
                        if kind == 0 and last:
                            (conv_mean, conv_centre, conv_rstd, conv_scale)[u](lay)

                if kind == 1 and part == 0:
                    dve.wait_ge(pv_done.sem, pv_done.at(lay, 16))
                    for v in (val_hi, val_lo):
                        f = f32(v[:, :, :, :])
                        dve.memset(f[:, 0, :, 64:P], 0.0)
                        o = dve.memset(f[:, 1, :, 0:64], 0.0)
                    o.then_inc(val_zeroed.sem, 1)
                if part == 0:
                    head(0, True, False)
                if part == 1:
                    with dve.Fori(1, KC - 1) as h:
                        head(h, False, False)
                if part < 2:
                    return
                head(KC - 1, False, True)
                if kind == 0:
                    conv_low(lay)
                turn_unit(KC, 0)
                if kind == 0:
                    gate_evict(lay, 0, KD - 1, 1, C_A + 2 * KD)
                else:
                    outs_ab(lay, KD - 1, 1)
                    outputs(KC - 1)

            dve.wait_ge(zeroed.sem, 3)
            for r in (0, 64):
                dve.memset(mask_q[r:r + 1, 0:64].bitcast(F32), 1.0).then_inc(consts.sem, 1)
                dve.memset(mask_k[r:r + 1, :].bitcast(F32), NEG_R).then_inc(consts.sem, 1)
            dve.wait_ge(lam_landed.sem, 16)
            lam = tmp[0][:, :].rearrange("p (l a b d) -> p l a b d", l=DEPTH, a=2, b=2)
            for l in range(DEPTH):
                for a in range(2):
                    o = dve.tensor_tensor(tmp[1][:, (2 * l + a) * 64:(2 * l + a) * 64 + 64], lam[:, l, a, 0, :],
                                          lam[:, l, a, 1, :], ALU.mult)
            o.then_inc(lam_prod.sem, 1)
            dve.wait_ge(lam_prod.sem, 1)
            dve.tensor_reduce(tmp[1][:, 256:256 + 2 * DEPTH], tmp[1][:, 0:256].rearrange("p (n d) -> p n d", d=64),
                              AX.X, ALU.add).then_inc(lam_prod.sem, 1)
            rel = ymix[0:DEPTH * HEADS_CHUNK, 0:2, :].rearrange("p a b -> p (a b)")
            dve.wait_ge(rel_landed.sem, 16)
            dve.memset(rel[:, EXT_LEFT + N_REL:EXT], 0.0).then_inc(rel_ready.sem, 1)
            dve.tensor_copy(rel[:, 0:EXT_LEFT], rel[:, EXT_LEFT:EXT_LEFT + 1].to_broadcast([DEPTH * HEADS_CHUNK, EXT_LEFT]))\
                .then_inc(rel_ready.sem, 1)
            dve.wait_ge(lam_done.sem, 1)
            for l in range(DEPTH):
                dve.tensor_scalar(neg_lam[:, l:l + 1], lam_exp[:, 2 * l + 1:2 * l + 2], lam_exp[:, 2 * l:2 * l + 1],
                                  -lam_init(l), ALU.subtract, ALU.add).then_inc(setup.sem, 1)
            dve.wait_ge(setup.sem, DEPTH)
            dve.wait_ge(par_landed.sem, 16)
            dve.wait_ge(consts.sem, N_CONSTS)
            dve.tensor_copy(ident_r[:, :], ident[:, :]).then_inc(ident_done.sem, 1)
            for s, k in ((pair_scaled, 4), (y_evicted, 2), (pt_ready, 1), (o_evicted, 1), (gate_evicted, 2), (out_evicted, 2)):
                dve.sem_inc(s.sem, k)

            with dve.Fori(0, DEPTH) as lay:
                dve.tensor_copy(pr[:, :], par_all[:, lay, :]).then_inc(par_copied.sem, 1)
                dve.wait_ge(par_copied.sem, par_copied.at(lay, 1))
                for k, n in ((KD, KD), (5 * KD, KD), (PAR_GATE_B, 3 * KD)):
                    dve.tensor_scalar(pr[:, k:k + n], pr[:, k:k + n], 0.5, None, ALU.mult).then_inc(par_copied.sem, 1)
                dve.wait_ge(par_copied.sem, par_copied.at(lay, 4))
                for t in range(KD):
                    h_low(lay, 0, t)
                sum_squares(lay, 0, squared, 0)
                norm_scalar(lay, 0)
                ffn(lay, 0, C_FFN1_IN, 0)
                residual(lay, 0)
                sum_squares(lay, 2, squared, KD)
                norm_scalar(lay, 2)
                glu(lay)
                rope_and_conv(lay)
                for part in range(3):
                    with dve.Fori(lay, lay + 1) as lay_a:
                        attention(lay_a, 0, C_A, part)
                chunk_qk(lay)
                for part in range(3):
                    with dve.Fori(lay, lay + 1) as lay_b:
                        attention(lay_b, 1, C_B, part)

                def last_branch(t, b):
                    gate_evict(lay, 2, t, b, C_C + 1 + t * 2)
                    dve.wait_ge(chunk_used.sem, chunk_used.at(lay, C_C + 2 + t * 2))
                    mix_next(lay, 2, t, b, acc[2 + b], t + 2 * KD)
                    dve.wait_ge(mix_hi_done.sem, mix_hi_done.at(lay, t + 1))
                    dve.scalar_tensor_tensor(mix_lo[:, t, :], ymix[:, t, :], 0.5, f32(mix_hi[:, t, :]),
                                             ALU.mult, ALU.subtract).then_inc(mix_ready.sem, 1)
                with dve.Fori(0, KD // 2) as i:
                    for e in range(2):
                        last_branch(i * 2 + e, e)
                sum_squares(lay, 3, y_squared, KD)
                norm_scalar(lay, 3)
                residual(lay, 1)
                sum_squares(lay, 4, squared, 2 * KD)
                norm_scalar(lay, 4)
                ffn(lay, 1, C_FFN2_IN, KF + KC)
                last_residual(lay)

        @block.tensor
        def _(pe):
            def products(slot, kk, xh, xl, out, start, stop):
                a = kk * P
                whi, wlo = w_hi[:, slot, a:a + P], w_lo[:, slot, a:a + P]
                pe.matmul(out, whi, xh, start=start, stop=False)
                pe.matmul(out, whi, xl, start=False, stop=False)
                return pe.matmul(out, wlo, xh, start=False, stop=stop)

            def split(lay, n):
                pe.wait_ge(split_done.sem, split_done.at(lay, n + 1))

            def chunk(lay, n, slot, k0, n_k, hi, lo, out, start, stop):
                split(lay, n)
                for kk in range(n_k):
                    o = products(slot, kk, hi[:, k0 + kk, :], lo[:, k0 + kk, :], out[:, :],
                                 start and kk == 0, stop and kk == n_k - 1)
                o.then_inc(chunk_used.sem, 1)

            def column_sums(src, signal, tiles, col, to=pv):
                for t in range(TT):
                    for i in range(tiles):
                        o = pe.matmul(to[:, col + t:col + t + 1], src(i)[:, t * P:(t + 1) * P], ones[:, 0:1],
                                      start=(i == 0), stop=(i == tiles - 1))
                if signal is not None:
                    o.then_inc(signal.sem, 1)

            def spread(signal, hi, lo, to=tr):
                for t in range(TT):
                    out = to[:, t * P:(t + 1) * P]
                    pe.matmul(out, hi[:, t:t + 1].to_broadcast([P, P]), ident_r[:, :], start=True, stop=False)
                    o = pe.matmul(out, lo[:, t:t + 1].to_broadcast([P, P]), ident_r[:, :], start=False, stop=True)
                o.then_inc(signal.sem, 1)

            def keep_warm(n):
                for _ in range(n):
                    pe.matmul(sc[0][:, :], ident_r[:, :], ident_r[:, :].unsqueeze(1).to_broadcast([P, TT, P]),
                              start=True, stop=True)

            def norm_behind(lay, k):
                keep_warm(7)
                norm_sums(lay, k)
                keep_warm(5)
                norm_spread(lay, k)
                keep_warm(18)

            def norm_sums(lay, k):
                pe.wait_ge(sq_added.sem, sq_added.at(lay, (k + 1) * KD))
                column_sums(lambda i: sqacc, summed, 1, 0)

            def norm_spread(lay, k):
                pe.wait_ge(parts_ready.sem, parts_ready.at(lay, k + 1))
                spread(bcast, r_hi, r_lo)

            def pairs(lay, c, first_pair, n_pairs, sub):
                def pair(e, j):
                    b = 2 * e
                    pe.wait_ge(pair_scaled.sem, pair_scaled.at(lay, (first_pair + j) * 2 - 2))
                    split(lay, c + j * 2 + 1)
                    for k in range(KD):
                        for half in range(2):
                            o = products(2 * e + half, k, h_hi[:, k, :], h_lo[:, k, :], acc[b + half][:, :],
                                         k == 0, k == KD - 1)
                            if k == KD - 1:
                                o.then_inc(chunk_used.sem, 1)

                pe.wait_ge(pair_scaled.sem, pair_scaled.at(lay, first_pair * 2))
                for k in range(KD):
                    pe.wait_ge(h_ready.sem, h_ready.at(lay, sub * KD + k + 1))
                    for m in range(3):
                        if k == 0:
                            split(lay, c + m)
                        o = products(m, k, h_hi[:, k, :], h_lo[:, k, :], acc[m][:, :], k == 0, k == KD - 1)
                        if k == KD - 1:
                            o.then_inc(chunk_used.sem, 1)
                split(lay, c + 3)
                for k in range(KD):
                    if k == 1:
                        norm_sums(lay, 2 * sub)
                    if k == 5:
                        norm_spread(lay, 2 * sub)
                    o = products(3, k, h_hi[:, k, :], h_lo[:, k, :], acc[3][:, :], k == 0, k == KD - 1)
                o.then_inc(chunk_used.sem, 1)
                with pe.Fori(1, n_pairs // 2) as i:
                    for e in range(2):
                        pair(e, i * 2 + e)

            def ffn_out_tiles(lay, sub, which, c, last_pair):
                def tile(t, e):
                    pe.wait_ge(pair_scaled.sem, pair_scaled.at(lay, last_pair * 2))
                    pe.wait_ge(y_evicted.sem, y_evicted.at(lay, sub * KD + t - 1))
                    for s, n_k in enumerate(FFN_OUT_K):
                        pe.wait_ge(act_ready.sem, act_ready.at(lay, which * KF + FFN_OUT_AT[s + 1]))
                        chunk(lay, c + t * RING + s, s, FFN_OUT_AT[s], n_k, act_hi, act_lo, acc[e], s == 0, s == RING - 1)
                with pe.Fori(0, KD // 2) as i:
                    for e in range(2):
                        tile(i * 2 + e, e)
                norm_behind(lay, 2 * sub + 1)

            def values(lay, c, emptied):
                for m in range(TT):
                    split(lay, c + m)
                    for t in range(TT):
                        for kk in range(2):
                            k = 2 * m + kk
                            whi = w_hi[:, m, kk * SEQ:(kk + 1) * SEQ]
                            wlo = w_lo[:, m, kk * SEQ:(kk + 1) * SEQ]
                            hh, hl = h_hi[:, k, t * P:(t + 1) * P], h_lo[:, k, t * P:(t + 1) * P]
                            if k == 0:
                                pe.wait_ge(emptied.sem, emptied.at(lay, KC + t + 1))
                            pe.matmul(acc[t][:, :], hh, whi, start=(k == 0), stop=False)
                            pe.matmul(acc[t][:, :], hh, wlo, start=False, stop=False)
                            o = pe.matmul(acc[t][:, :], hl, whi, start=False, stop=(k == KD - 1))
                    o.then_inc(chunk_used.sem, 1)

            def attention(lay, kind, c, c_next):
                U0, H0, S0, T0 = 16 * kind, KC * kind, 32 * kind, 16 * kind
                n_comp = 1 + kind

                def scores(h, u):
                    w = (u + 1) * P
                    if u == 0:
                        pe.wait_ge(qk_staged.sem, qk_staged.at(lay, h + (H0 + 1)))
                    for comp in range(2):
                        r = slice(64 * comp, 64 * comp + 64)
                        pe.wait_ge(exp_done.sem, exp_done.at(lay, h * 8 + (S0 + 2 * u + comp - 1)))
                        qh, ql = q_hi[r, u * P:w], q_lo[r, u * P:w]
                        out = sc[comp][:, 0:w]
                        pe.matmul(out, qh, k_hi[r, 0:w], start=True, stop=False)
                        pe.matmul(out, qh, k_lo[r, 0:w], start=False, stop=False)
                        pe.matmul(out, ql, k_hi[r, 0:w], start=False, stop=False)
                        pe.matmul(sc[comp][:, w - 64:w], mask_q[r, :], mask_k[r, :], start=False, stop=True)\
                            .then_inc(scores_done.sem, 1)

                def turn(h, u, comp):
                    hp, up = (h, u - 1) if u else (h - 1, 3)
                    m = (hp * 4 + up) * n_comp + (T0 + comp)
                    pe.wait_ge(prob_ready.sem, prob_ready.at(lay, hp * 4 + (U0 + up + 1)))
                    pe.wait_ge(pt_ready.sem, pt_ready.at(lay, m))
                    for j in range(up + 1):
                        o = pe.transpose(tr[:, j * P:(j + 1) * P], prob[:, up % 2, comp, j * P:(j + 1) * P], ident[:, :])
                    o.then_inc(turned.sem, 1)

                def weigh(h, u):
                    hp, up = (h, u - 2) if u >= 2 else (h - 1, u + 2)
                    m = (hp * 4 + up) * n_comp + (T0 + n_comp)
                    if up == 0:
                        pe.wait_ge(val_staged.sem, val_staged.at(lay, hp + (H0 + 1)))
                        pe.wait_ge(o_evicted.sem, o_evicted.at(lay, hp + H0))
                        if kind == 1:
                            pe.wait_ge(val_zeroed.sem, val_zeroed.at(lay, 1))
                    pe.wait_ge(pt_ready.sem, pt_ready.at(lay, m))
                    n = n_comp * (up + 1) * 3
                    i = 0
                    for comp in range(n_comp):
                        for j in range(up + 1):
                            for a, b in ((val_hi, pt_hi), (val_hi, pt_lo), (val_lo, pt_hi)):
                                o = pe.matmul(pv[:, up * P:(up + 1) * P], a[:, comp, j, :], b[:, comp, j, :],
                                              start=(i == 0), stop=(i == n - 1))
                                i += 1
                    o.then_inc(pv_done.sem, 1)

                def half(slot, at, k0, hi, lo, bank_, opens, closes):
                    for k in range(KC):
                        o = products(slot, at + k, hi[:, k0 + k, :], lo[:, k0 + k, :], bank_[:, :],
                                     opens and k == 0, closes and k == KC - 1)
                    return o

                def dense(h, u, part):
                    t = h * 2 + u // 2
                    e = u // 2
                    first_half = u % 2 == 0
                    if kind == 0:
                        if part == 0:
                            if first_half:
                                pe.wait_ge(gate_evicted.sem, gate_evicted.at(lay, t - 1))
                            split(lay, c + h * 4 + u)
                            half(u, 0, 0 if first_half else KC, h_hi, h_lo, acc[e], first_half, not first_half)\
                                .then_inc(chunk_used.sem, 1)
                    elif first_half:
                        if part == 0:
                            pe.wait_ge(gate_evicted.sem, gate_evicted.at(lay, t + (KD - 1)))
                            split(lay, c + t * 2)
                            half(2 * e, 0, 0, h_hi, h_lo, acc[e], True, False)
                        else:
                            half(2 * e, KC, KC, h_hi, h_lo, acc[e], False, True).then_inc(chunk_used.sem, 1)
                    elif part == 0:
                        pe.wait_ge(out_evicted.sem, out_evicted.at(lay, t * 2 - 1))
                        pe.wait_ge(u_ready.sem, u_ready.at(lay, KC))
                        split(lay, c + t * 2 + 1)
                        half(2 * e + 1, 0, 0, conv_hi, conv_lo, acc[2], True, True)
                    else:
                        pe.wait_ge(out_evicted.sem, out_evicted.at(lay, t * 2))
                        pe.wait_ge(u_ready.sem, u_ready.at(lay, 2 * KC))
                        half(2 * e + 1, KC, 0, diff_hi, diff_lo, acc[3], True, True).then_inc(chunk_used.sem, 1)

                def conv_norm(u, before):
                    if u == 0 and not before:
                        pe.wait_ge(tap_done.sem, tap_done.at(lay, KC * (CONV_K + 1)))
                        column_sums(lambda i: conv_raw[:, i, :], ln_sums, KC, 0, acc[2])
                    if u in (1, 3) and before:
                        pe.wait_ge(ln_parts.sem, ln_parts.at(lay, (u + 1) // 2))
                        spread(ln_bcast, r2_hi, r2_lo, acc[3])
                    if u == 2 and not before:
                        pe.wait_ge(ln_squared.sem, ln_squared.at(lay, KC))
                        column_sums(lambda i: conv_sq[:, i, :], ln_sums, KC, 0, acc[2])

                def head(h, first, last):
                    for u in range(4):
                        scores(h, u)
                        if u >= 2 or not first:
                            weigh(h, u)
                        if u or not first:
                            turn(h, u, 0)
                        if first and u in (0, 1):
                            pe.wait_ge(v_evicted.sem, v_evicted.at(lay, TT * kind + (TT if u else 1)))
                        if kind == 0 and last:
                            conv_norm(u, True)
                        dense(h, u, 0)
                        if kind == 1 and (u or not first):
                            turn(h, u, 1)
                        dense(h, u, 1)
                        if kind == 0 and last:
                            conv_norm(u, False)

                head(0, True, False)
                with pe.Fori(1, KC - 1) as h:
                    head(h, False, False)
                head(KC - 1, False, True)
                weigh(KC, 0)
                turn(KC, 0, 0)
                pe.wait_ge(gate_evicted.sem, gate_evicted.at(lay, KD * (kind + 1) - 1))
                split(lay, c_next)
                half(0, 0, 0, h_hi, h_lo, acc[0], True, False)
                if kind == 1:
                    turn(KC, 0, 1)
                half(0, KC, KC, h_hi, h_lo, acc[0], False, True).then_inc(chunk_used.sem, 1)
                weigh(KC, 1)

            pe.wait_ge(consts.sem, N_CONSTS)
            pe.wait_ge(ident_done.sem, 1)
            keep_warm(30)
            for s, k in ((chunk_used, RING), (pv_done, 1)):
                pe.sem_inc(s.sem, k)

            with pe.Fori(0, DEPTH) as lay:
                pairs(lay, C_FFN1_IN, 0, KF, 0)
                ffn_out_tiles(lay, 0, 0, C_FFN1_OUT, KF - 1)
                pairs(lay, C_GLU, KF, KC, 1)
                for j in range(2 * KC):
                    if j < 4:
                        pe.wait_ge(pair_scaled.sem, pair_scaled.at(lay, 2 * (KF + KC) - (2 if j < 2 else 0)))
                    else:
                        pe.wait_ge(cos_part.sem, cos_part.at(lay, j - 3))
                    chunk(lay, C_DQK + j, j % RING, 0, KD, h_hi, h_lo, acc[j % 4], True, True)
                values(lay, C_DV, cos_part)
                attention(lay, 0, C_A, C_CQK)
                for j in range(2 * KC):
                    if j == 1:
                        pe.wait_ge(gate_evicted.sem, gate_evicted.at(lay, KD))
                    if j >= 4:
                        pe.wait_ge(cqk_evicted.sem, cqk_evicted.at(lay, j - 3))
                    if j:
                        chunk(lay, C_CQK + j, j % RING, 0, KD, h_hi, h_lo, acc[j % 4], True, True)
                    if j == 0:
                        pe.wait_ge(o_evicted.sem, o_evicted.at(lay, KC))
                        for h in range(KC):
                            column_sums(lambda i: diff_sq[:, KC - 1 - h, :], dn_sums if h == KC - 1 else None, 1, 4 * h)
                    elif j <= KC:
                        if j == 1:
                            pe.wait_ge(dn_parts.sem, dn_parts.at(lay, 1))
                        else:
                            pe.wait_ge(dn_normed.sem, dn_normed.at(lay, j - 1))
                        spread(dn_bcast, r2_hi[:, 4 * (j - 1):4 * j], r2_lo[:, 4 * (j - 1):4 * j])
                values(lay, C_CV, cqk_evicted)
                attention(lay, 1, C_B, C_C)

                def gate_c(t, e):
                    pe.wait_ge(gate_evicted.sem, gate_evicted.at(lay, t + (2 * KD - 1)))
                    chunk(lay, C_C + t * 2, 2 * e, 0, KD, h_hi, h_lo, acc[e], True, True)

                def out_c_tile(t, e):
                    pe.wait_ge(o_evicted.sem, o_evicted.at(lay, 2 * KC))
                    pe.wait_ge(out_evicted.sem, out_evicted.at(lay, t + (2 * KD - 1)))
                    chunk(lay, C_C + t * 2 + 1, 2 * e + 1, 0, KC, chunk_hi, chunk_lo, acc[2 + e], True, True)

                out_c_tile(0, 0)
                gate_c(1, 1)
                out_c_tile(1, 1)
                with pe.Fori(1, KD // 2) as i:
                    for e in range(2):
                        gate_c(i * 2 + e, e)
                        out_c_tile(i * 2 + e, e)
                pe.wait_ge(gate_evicted.sem, gate_evicted.at(lay, 3 * KD))
                for t in range(KD):
                    pe.wait_ge(y_evicted.sem, y_evicted.at(lay, KD + t - 1))
                    split(lay, C_WO + t)
                    for k in range(KD):
                        if t == 0:
                            pe.wait_ge(mix_ready.sem, mix_ready.at(lay, k + 1))
                        o = products(t % RING, k, mix_hi[:, k, :], mix_lo[:, k, :], acc[t % 2][:, :], k == 0, k == KD - 1)
                    o.then_inc(chunk_used.sem, 1)
                norm_behind(lay, 3)
                pairs(lay, C_FFN2_IN, KF + KC, KF, 2)
                ffn_out_tiles(lay, 2, 1, C_FFN2_OUT, 2 * KF + KC - 1)


def tiles(w, n_k):
    k, n = w.shape
    return w.reshape(n_k, P, n // P, P).transpose(2, 1, 0, 3).reshape(n // P, P, n_k * P)


def kernel(x, norm_g, ffn1_in, ffn1_out, w_in, gate_b, conv_dw, conv_b, conv_ln, w_conv_out, diff_lambda,
           w_diff_out, rel_bias, w_chunk_out, w_o, ffn2_in, ffn2_out):
    import concourse.bacc as _bacc
    from concourse.bass_utils import run_bass_kernel_spmd as _run

    a = {k: np.asarray(v) for k, v in dict(
        x=x, norm_g=norm_g, ffn1_in=ffn1_in, ffn1_out=ffn1_out, w_in=w_in, gate_b=gate_b, conv_dw=conv_dw,
        conv_b=conv_b, conv_ln=conv_ln, w_conv_out=w_conv_out, diff_lambda=diff_lambda, w_diff_out=w_diff_out,
        rel_bias=rel_bias, w_chunk_out=w_chunk_out, w_o=w_o, ffn2_in=ffn2_in, ffn2_out=ffn2_out).items()}

    ffn_in_t, ffn_out_t, mix_t, ab_t, c_t, wo_t, par_t = [], [], [], [], [], [], []
    for l in range(DEPTH):
        for f in ("ffn1", "ffn2"):
            t = tiles(a[f + "_in"][l], KD)
            ffn_in_t.append(np.stack([t[:KF], t[KF:]], axis=1).reshape(2 * KF, P, CHUNK))
            ffn_out_t.append(tiles(a[f + "_out"][l], KF))
        t = tiles(a["w_in"][l], KD)
        o_glu, o_dq, o_dk, o_dv, o_cq, o_ck, o_cv, o_gate = 0, 8, 12, 16, 20, 24, 28, 32

        def value_chunks(o):
            w = a["w_in"][l][:, o * P:o * P + SEQ]
            return w.reshape(TT, 2, P, SEQ).transpose(0, 2, 1, 3).reshape(TT, P, CHUNK)

        glu = np.stack([t[o_glu:o_glu + KC], t[o_glu + KC:o_dq]], axis=1).reshape(2 * KC, P, CHUNK)
        mix_t.append(np.concatenate([
            glu, t[o_dq:o_dv], value_chunks(o_dv), t[o_gate:o_gate + KD],
            t[o_cq:o_cv], value_chunks(o_cv), t[o_gate + KD:o_gate + 3 * KD]]))
        ab_t.append(np.concatenate([tiles(a[n][l], KC) for n in ("w_conv_out", "w_diff_out")], axis=2))
        c_t.append(tiles(a["w_chunk_out"][l], KC))
        wo_t.append(tiles(a["w_o"][l], KD))
        cols = [a["norm_g"][l].reshape(6 * KD, P), a["gate_b"][l].reshape(3 * KD, P),
                a["conv_dw"][l].reshape(CONV_K, KC, P).transpose(1, 0, 2).reshape(KC * CONV_K, P),
                a["conv_b"][l].reshape(KC, P), a["conv_ln"][l].reshape(2 * KC, P)]
        par_t.append(np.concatenate(cols).T)

    inv = (np.float32(10000.0) ** (-np.arange(0, 64, 2, dtype=np.float32) / np.float32(64))).astype(np.float32)
    ang = np.arange(SEQ, dtype=np.float32)[:, None] * inv[None, :]
    cos, sin = np.cos(ang).T.astype(np.float32), np.sin(ang).T.astype(np.float32)
    rope = np.stack([np.concatenate([cos] * 4), np.concatenate([-sin, sin] * 2)])

    arrays = {
        "xT": a["x"][0].T.reshape(KD, P, SEQ).transpose(1, 0, 2),
        "ffn_in": np.concatenate(ffn_in_t), "ffn_out": np.concatenate(ffn_out_t),
        "mix_in": np.concatenate(mix_t), "out_ab": np.concatenate(ab_t),
        "out_c": np.concatenate(c_t), "wo": np.concatenate(wo_t),
        "par": np.stack(par_t, axis=1),
        "lamb": a["diff_lambda"].reshape(DEPTH * 4 * 64),
        "relb": a["rel_bias"][:, :, ::-1].reshape(DEPTH * HEADS_CHUNK, N_REL),
        "rope": rope,
    }
    arrays = {k: np.ascontiguousarray(v) for k, v in arrays.items()}
    nc = _bacc.Bacc("TRN2", target_bir_lowering=False, num_devices=1, dynamic_dma_scratch_size=1024)
    args = [nc.dram_tensor(k, v.shape, mybir.dt.from_np(v.dtype), kind="ExternalInput").ap() for k, v in arrays.items()]
    args.append(nc.dram_tensor("outT", (P, KD, SEQ), F32, kind="ExternalOutput").ap())
    build(nc, *args)
    r = _run(nc, [arrays], core_ids=[0])
    out = np.asarray(r.results[0]["outT"])
    return np.ascontiguousarray(out.transpose(1, 0, 2).reshape(D_MODEL, SEQ).T).reshape(1, SEQ, D_MODEL)
```
